# Optimizing a Trainium2 kernel written in Bass

```python
import jax
import jax.numpy as jnp
from jax import lax
import numpy as np
import math
import jax, jax.numpy as jnp

D_MODEL = 1024
BATCH = 1
SEQ = 256
DEPTH = 1

CHUNK = 64
Q_BLOCK = 128
N_MEM = 256
EPS = 1e-6
SB_HD = 128
SB_HEADS = D_MODEL // SB_HD
SB_W = SB_HEADS * SB_HD
ML_HEADS = 4
ML_HD = D_MODEL // ML_HEADS
ML_W = ML_HEADS * ML_HD
X_HEADS = 4
X_HD = D_MODEL // X_HEADS
X_W = X_HEADS * X_HD
CONV_W = 4
D_FF = 4 * D_MODEL
N_BRANCH = 3
IN_SIZES = (SB_W, SB_W, SB_W, ML_W, ML_W, ML_W, ML_W, ML_HEADS, ML_HEADS, X_W, N_BRANCH * D_MODEL)
IN_SPLITS = tuple(int(v) for v in np.cumsum(IN_SIZES)[:-1])
N_IN = int(sum(IN_SIZES))


def _rmsnorm(x, g):
    xf = x.astype(jnp.float32)
    y = xf * lax.rsqrt(jnp.mean(xf * xf, axis=-1, keepdims=True) + EPS)
    return (y * g.astype(jnp.float32)).astype(x.dtype)

def _split_heads(t, n):
    b, s, _ = t.shape
    return t.reshape(b, s, n, -1).transpose(0, 2, 1, 3)

def _merge_heads(t):
    b, h, s, d = t.shape
    return t.transpose(0, 2, 1, 3).reshape(b, s, h * d)

def _causal_conv(u, w, b):
    s = u.shape[1]
    up = jnp.pad(u, ((0, 0), (CONV_W - 1, 0), (0, 0)))
    return sum((up[:, j:j + s, :] * w[j] for j in range(CONV_W)), b)

def _stick_breaking(q, k, v):
    _, _, s_len, dh = q.shape
    scale = dh ** -0.5
    kf = k.astype(jnp.float32)
    vf = v.astype(jnp.float32)
    outs = []
    for blk in range(s_len // Q_BLOCK):
        start, end = blk * Q_BLOCK, (blk + 1) * Q_BLOCK
        qb = q[:, :, start:end].astype(jnp.float32)
        z = jnp.einsum('bhqd,bhkd->bhqk', qb, kf[:, :, :end]) * scale
        q_pos = start + jnp.arange(Q_BLOCK)
        k_pos = jnp.arange(end)
        causal = k_pos[None, :] < q_pos[:, None]
        log_1m = jnp.where(causal, jax.nn.log_sigmoid(-z), 0.0)
        later = lax.cumsum(log_1m, axis=3, reverse=True) - log_1m
        log_a = jnp.where(causal, jax.nn.log_sigmoid(z) + later, -jnp.inf)
        outs.append(jnp.einsum('bhqk,bhkd->bhqd', jnp.exp(log_a), vf[:, :, :end]))
    return jnp.concatenate(outs, axis=2)

def _mlstm(q, k, v, i_pre, f_pre):
    f32 = jnp.float32
    b, h, s_len, dh = q.shape
    nc = s_len // CHUNK
    q = q.astype(f32)
    k = k.astype(f32) * (dh ** -0.5)
    v = v.astype(f32)
    i_pre = i_pre.astype(f32)
    log_f = jax.nn.log_sigmoid(f_pre.astype(f32))

    def chunks(t):
        return jnp.moveaxis(t.reshape(b, h, nc, CHUNK, *t.shape[3:]), 2, 0)

    tri = jnp.tril(jnp.ones((CHUNK, CHUNK), dtype=bool))

    def step(carry, xs):
        c_prev, n_prev, m_prev = carry
        qc, kc, vc, ic, lfc = xs
        bcum = jnp.cumsum(lfc, axis=-1)
        d = jnp.where(tri, bcum[..., :, None] - bcum[..., None, :] + ic[..., None, :], -jnp.inf)
        m_inter = bcum + m_prev[..., None]
        m_t = jnp.maximum(m_inter, jnp.max(d, axis=-1))
        w = jnp.exp(d - m_t[..., None])
        s_inter = jnp.exp(m_inter - m_t)
        sc = jnp.einsum('bhtd,bhsd->bhts', qc, kc) * w
        num = jnp.einsum('bhts,bhsd->bhtd', sc, vc) + s_inter[..., None] * jnp.einsum('bhvk,bhtk->bhtv', c_prev, qc)
        den = jnp.sum(sc, axis=-1) + s_inter * jnp.einsum('bhtk,bhk->bht', qc, n_prev)
        h_c = num / jnp.maximum(jnp.abs(den), jnp.exp(-m_t))[..., None]
        b_end = bcum[..., -1]
        g = b_end[..., None] - bcum + ic
        m_new = jnp.maximum(b_end + m_prev, jnp.max(g, axis=-1))
        decay = jnp.exp(b_end + m_prev - m_new)
        wk = jnp.exp(g - m_new[..., None])
        c_new = decay[..., None, None] * c_prev + jnp.einsum('bhsv,bhsk->bhvk', vc * wk[..., None], kc)
        n_new = decay[..., None] * n_prev + jnp.einsum('bhs,bhsk->bhk', wk, kc)
        return (c_new, n_new, m_new), h_c

    init = (jnp.zeros((b, h, dh, dh), f32), jnp.zeros((b, h, dh), f32), jnp.zeros((b, h), f32))
    _, hs = lax.scan(step, init, (chunks(q), chunks(k), chunks(v), chunks(i_pre), chunks(log_f)))
    return jnp.moveaxis(hs, 0, 2).reshape(b, h, s_len, dh)

def _cross_attention(q, mk, mv, gq, gk):
    dh = q.shape[-1]
    qn = _rmsnorm(q, gq)
    kn = _rmsnorm(mk, gk)
    logits = jnp.einsum('bhsd,bhmd->bhsm', qn, kn).astype(jnp.float32) * (dh ** -0.5)
    p = jax.nn.softmax(logits, axis=-1)
    return jnp.einsum('bhsm,bhmd->bhsd', p.astype(mv.dtype), mv)

def first_inputs(seed: int = 0) -> dict:
    key = jax.random.key(seed)
    ks = jax.random.split(key, 24)
    f32 = jnp.float32
    L = DEPTH

    def nrm(k, shape, scale):
        return jax.random.normal(k, shape, f32) * scale

    def gain(k, shape):
        return 1.0 + 0.02 * jax.random.normal(k, shape, f32)

    b_i = nrm(ks[4], (L, ML_HEADS), 0.1)
    b_f = jnp.linspace(3.0, 6.0, ML_HEADS, dtype=f32)[None, :] + nrm(ks[5], (L, ML_HEADS), 0.1)
    return {
        "x": nrm(ks[0], (BATCH, SEQ, D_MODEL), 1.0),
        "mem": nrm(ks[1], (BATCH, N_MEM, D_MODEL), 1.0),
        "g_mix": gain(ks[2], (L, D_MODEL)),
        "w_in": nrm(ks[3], (L, D_MODEL, N_IN), D_MODEL ** -0.5),
        "b_if": jnp.concatenate([b_i, b_f], axis=-1),
        "b_gate": nrm(ks[6], (L, N_BRANCH * D_MODEL), 0.02),
        "conv_w": nrm(ks[7], (L, CONV_W, 2 * ML_W), CONV_W ** -0.5),
        "conv_b": nrm(ks[8], (L, 2 * ML_W), 0.02),
        "ml_norm_g": gain(ks[9], (L, ML_W)),
        "g_mem": gain(ks[10], (L, D_MODEL)),
        "w_mem_kv": nrm(ks[11], (L, D_MODEL, 2 * X_W), D_MODEL ** -0.5),
        "q_norm_g": gain(ks[12], (L, X_HD)),
        "k_norm_g": gain(ks[13], (L, X_HD)),
        "w_sb_proj": nrm(ks[14], (L, SB_W, D_MODEL), SB_W ** -0.5),
        "w_ml_proj": nrm(ks[15], (L, ML_W, D_MODEL), ML_W ** -0.5),
        "w_x_proj": nrm(ks[16], (L, X_W, D_MODEL), X_W ** -0.5),
        "w_out": nrm(ks[17], (L, D_MODEL, D_MODEL), D_MODEL ** -0.5),
        "g_mlp": gain(ks[18], (L, D_MODEL)),
        "w_ff1": nrm(ks[19], (L, D_MODEL, D_FF), D_MODEL ** -0.5),
        "w_ff2": nrm(ks[20], (L, D_FF, D_MODEL), D_FF ** -0.5),
    }

def first_block(x, mem, g_mix, w_in, b_if, b_gate, conv_w, conv_b, ml_norm_g, g_mem, w_mem_kv,
              q_norm_g, k_norm_g, w_sb_proj, w_ml_proj, w_x_proj, w_out, g_mlp, w_ff1, w_ff2):
    dt = x.dtype
    bsz, seq, _ = x.shape
    for l in range(DEPTH):
        h = _rmsnorm(x, g_mix[l])
        z = h @ w_in[l]
        (sb_q, sb_k, sb_v, ml_q, ml_k, ml_v, ml_o, ml_i, ml_f, x_q, gate_pre) = jnp.split(z, IN_SPLITS, axis=-1)

        y_sb = _merge_heads(_stick_breaking(_split_heads(sb_q, SB_HEADS), _split_heads(sb_k, SB_HEADS),
                                            _split_heads(sb_v, SB_HEADS))).astype(dt)

        qk = jax.nn.silu(_causal_conv(jnp.concatenate([ml_q, ml_k], axis=-1), conv_w[l], conv_b[l]))
        mq, mk = jnp.split(qk, 2, axis=-1)
        i_pre = (ml_i + b_if[l, :ML_HEADS]).transpose(0, 2, 1)
        f_pre = (ml_f + b_if[l, ML_HEADS:]).transpose(0, 2, 1)
        hm = _mlstm(_split_heads(mq, ML_HEADS), _split_heads(mk, ML_HEADS), _split_heads(ml_v, ML_HEADS), i_pre, f_pre)
        hm = _rmsnorm(hm, ml_norm_g[l].reshape(ML_HEADS, 1, ML_HD))
        y_ml = (_merge_heads(hm) * jax.nn.sigmoid(ml_o.astype(jnp.float32))).astype(dt)

        kv = _rmsnorm(mem, g_mem[l]) @ w_mem_kv[l]
        mem_k, mem_v = jnp.split(kv, 2, axis=-1)
        y_x = _merge_heads(_cross_attention(_split_heads(x_q, X_HEADS), _split_heads(mem_k, X_HEADS),
                                            _split_heads(mem_v, X_HEADS), q_norm_g[l], k_norm_g[l])).astype(dt)

        gates = jax.nn.sigmoid(gate_pre + b_gate[l]).reshape(bsz, seq, N_BRANCH, D_MODEL)
        mixed = (gates[:, :, 0] * (y_sb @ w_sb_proj[l])
                 + gates[:, :, 1] * (y_ml @ w_ml_proj[l])
                 + gates[:, :, 2] * (y_x @ w_x_proj[l]))
        x = x + mixed @ w_out[l]

        u = _rmsnorm(x, g_mlp[l]) @ w_ff1[l]
        x = x + jnp.square(jax.nn.relu(u)) @ w_ff2[l]
    return x


HEAD_DIM = 64
N_ATT_HEADS = 12
ATT_WIDTH = N_ATT_HEADS * HEAD_DIM
DILATED_PATTERNS = ((128, 1), (512, 4), (2048, 16))
ATT_BLOCK = 128
SSM_EXPAND = 2
SSM_INNER = SSM_EXPAND * D_MODEL
SSM_HEAD_DIM = 64
SSM_HEADS = SSM_INNER // SSM_HEAD_DIM
SSM_GROUPS = 8
SSM_STATE = 128
SSM_CONV = 4
SSM_CHUNK = 128
CONV_DIM = SSM_INNER + 2 * SSM_GROUPS * SSM_STATE
FFN_HIDDEN = 4 * D_MODEL
N_BRANCHES = 2
IN_SPLITS_2 = (ATT_WIDTH, ATT_WIDTH, ATT_WIDTH, SSM_INNER, CONV_DIM, SSM_HEADS, N_BRANCHES * D_MODEL)
IN_PROJ_WIDTH = sum(IN_SPLITS_2)
RMS_EPS = 1e-6


def rmsnorm(x, w):
    x32 = x.astype(jnp.float32)
    y = x32 * lax.rsqrt(jnp.mean(x32 * x32, axis=-1, keepdims=True) + RMS_EPS)
    return (y * w.astype(jnp.float32)).astype(x.dtype)

def alibi_slopes(n):
    def pow2(m):
        start = 2.0 ** (-8.0 / m)
        return [start ** (i + 1) for i in range(m)]
    if (n & (n - 1)) == 0:
        s = pow2(n)
    else:
        c = 2 ** int(math.floor(math.log2(n)))
        s = pow2(c) + pow2(2 * c)[0::2][: n - c]
    return jnp.asarray(np.array(s, dtype=np.float32))

def dilated_window_attention(q, k, v, slopes, window, dilation):
    b, s, h, dh = q.shape
    band = window // dilation
    blk = ATT_BLOCK
    span = dilation * blk
    s_pad = -(-s // span) * span
    pad = ((0, 0), (0, s_pad - s), (0, 0), (0, 0))
    q, k, v = [jnp.pad(t, pad) for t in (q, k, v)]
    nb = s_pad // span
    qb = q.reshape(b, nb, blk, dilation, h, dh)
    kb = k.reshape(b, nb, blk, dilation, h, dh)
    vb = v.reshape(b, nb, blk, dilation, h, dh)

    def with_prev(t):
        prev = jnp.concatenate([jnp.zeros_like(t[:, :1]), t[:, :-1]], axis=1)
        return jnp.concatenate([prev, t], axis=2)

    kk, vv = with_prev(kb), with_prev(vb)
    scores = jnp.einsum('bnirhd,bnjrhd->bnrhij', qb, kk,
                        preferred_element_type=jnp.float32) * (dh ** -0.5)
    i_idx = jnp.arange(blk)[:, None]
    j_idx = jnp.arange(2 * blk)[None, :]
    dist = blk + i_idx - j_idx
    n_idx = jnp.arange(nb)[:, None, None]
    valid = (dist >= 0) & (dist <= band) & ((n_idx > 0) | (j_idx >= blk))
    bias = -slopes[:, None, None] * (dist * dilation).astype(jnp.float32)
    scores = scores + bias[None, None, None]
    scores = jnp.where(valid[None, :, None, None], scores, -jnp.inf)
    m = jnp.max(scores, axis=-1, keepdims=True)
    p = jnp.exp(scores - m)
    l = jnp.sum(p, axis=-1)
    o = jnp.einsum('bnrhij,bnjrhd->bnirhd', p, vv.astype(jnp.float32))
    l_t = jnp.transpose(l, (0, 1, 4, 2, 3))
    m_t = jnp.transpose(m[..., 0], (0, 1, 4, 2, 3))
    o = o / l_t[..., None]
    o = o.reshape(b, s_pad, h, dh)[:, :s]
    return o, m_t.reshape(b, s_pad, h)[:, :s], l_t.reshape(b, s_pad, h)[:, :s]

def ssd_chunked(x, dt, a, bmat, cmat):
    b, s, g, hg, p = x.shape
    n = bmat.shape[-1]
    ch = SSM_CHUNK
    s_pad = -(-s // ch) * ch
    padlen = s_pad - s
    x = jnp.pad(x.astype(jnp.float32), ((0, 0), (0, padlen), (0, 0), (0, 0), (0, 0)))
    dt = jnp.pad(dt, ((0, 0), (0, padlen), (0, 0), (0, 0)))
    bmat = jnp.pad(bmat.astype(jnp.float32), ((0, 0), (0, padlen), (0, 0), (0, 0)))
    cmat = jnp.pad(cmat.astype(jnp.float32), ((0, 0), (0, padlen), (0, 0), (0, 0)))
    c = s_pad // ch
    xd = (x * dt[..., None]).reshape(b, c, ch, g, hg, p)
    la = jnp.moveaxis((dt * a).reshape(b, c, ch, g, hg), 2, -1)
    bc = bmat.reshape(b, c, ch, g, n)
    cc = cmat.reshape(b, c, ch, g, n)
    a_cs = jnp.cumsum(la, axis=-1)
    tril = jnp.tril(jnp.ones((ch, ch), dtype=bool))
    decay = jnp.exp(jnp.where(tril, a_cs[..., :, None] - a_cs[..., None, :], -jnp.inf))
    cb = jnp.einsum('bclgn,bcsgn->bcgls', cc, bc)
    y_diag = jnp.einsum('bcghls,bcsghp->bclghp', cb[:, :, :, None] * decay, xd)
    decay_states = jnp.exp(a_cs[..., -1:] - a_cs)
    states = jnp.einsum('bclgn,bcghl,bclghp->bcghpn', bc, decay_states, xd)
    chunk_decay = jnp.exp(a_cs[..., -1])

    def step(hstate, inp):
        st, dec = inp
        return hstate * dec[..., None, None] + st, hstate

    init = jnp.zeros((b, g, hg, p, n), jnp.float32)
    _, prev = lax.scan(step, init, (jnp.moveaxis(states, 1, 0), jnp.moveaxis(chunk_decay, 1, 0)))
    prev = jnp.moveaxis(prev, 0, 1)
    y_off = jnp.einsum('bclgn,bcghpn,bcghl->bclghp', cc, prev, jnp.exp(a_cs))
    return (y_diag + y_off).reshape(b, s_pad, g, hg, p)[:, :s]

def mamba2_mixer(z, xbc, dt_raw, conv_w, conv_b, dt_bias, a_log, d_skip, norm_w):
    b, s, _ = z.shape
    hg = SSM_HEADS // SSM_GROUPS
    xbc = lax.conv_general_dilated(xbc, conv_w[:, None, :], window_strides=(1,),
                                   padding=[(SSM_CONV - 1, 0)],
                                   dimension_numbers=('NWC', 'WIO', 'NWC'),
                                   feature_group_count=CONV_DIM) + conv_b
    xbc = jax.nn.silu(xbc)
    xs, bm, cm = jnp.split(xbc, [SSM_INNER, SSM_INNER + SSM_GROUPS * SSM_STATE], axis=-1)
    xh = xs.reshape(b, s, SSM_GROUPS, hg, SSM_HEAD_DIM)
    bm = bm.reshape(b, s, SSM_GROUPS, SSM_STATE)
    cm = cm.reshape(b, s, SSM_GROUPS, SSM_STATE)
    dt = jax.nn.softplus((dt_raw + dt_bias).astype(jnp.float32)).reshape(b, s, SSM_GROUPS, hg)
    a = -jnp.exp(a_log.astype(jnp.float32)).reshape(SSM_GROUPS, hg)
    y = ssd_chunked(xh, dt, a, bm, cm)
    y = y + d_skip.astype(jnp.float32).reshape(SSM_GROUPS, hg)[:, :, None] * xh.astype(jnp.float32)
    y = y.reshape(b, s, SSM_INNER) * jax.nn.silu(z.astype(jnp.float32))
    yg = y.reshape(b, s, SSM_GROUPS, SSM_INNER // SSM_GROUPS)
    yg = yg * lax.rsqrt(jnp.mean(yg * yg, axis=-1, keepdims=True) + RMS_EPS)
    y = yg.reshape(b, s, SSM_INNER) * norm_w.astype(jnp.float32)
    return y.astype(z.dtype)

def second_inputs(seed: int = 0) -> dict:
    key = jax.random.key(seed)
    ks = jax.random.split(key, 20)
    f32 = jnp.float32

    def nrm(k, shape, scale):
        return jax.random.normal(k, shape, f32) * scale

    def gain(k, width):
        return 1.0 + 0.05 * jax.random.normal(k, (DEPTH, width), f32)

    dt0 = jnp.exp(jax.random.uniform(ks[7], (DEPTH, SSM_HEADS), f32,
                                     math.log(1e-3), math.log(1e-1)))
    return {
        "x": jax.random.normal(ks[0], (BATCH, SEQ, D_MODEL), f32),
        "norm_mix_pre_w": gain(ks[1], D_MODEL),
        "w_in": nrm(ks[2], (DEPTH, D_MODEL, IN_PROJ_WIDTH), D_MODEL ** -0.5),
        "b_gate": nrm(ks[3], (DEPTH, N_BRANCHES * D_MODEL), 0.02),
        "conv_w": nrm(ks[4], (DEPTH, SSM_CONV, CONV_DIM), SSM_CONV ** -0.5),
        "conv_b": nrm(ks[5], (DEPTH, CONV_DIM), 0.02),
        "dt_bias": dt0 + jnp.log(-jnp.expm1(-dt0)),
        "a_log": jnp.log(jax.random.uniform(ks[8], (DEPTH, SSM_HEADS), f32, 1.0, 16.0)),
        "d_skip": 1.0 + 0.1 * jax.random.normal(ks[9], (DEPTH, SSM_HEADS), f32),
        "ssm_norm_w": gain(ks[10], SSM_INNER),
        "w_att_proj": nrm(ks[11], (DEPTH, ATT_WIDTH, D_MODEL), ATT_WIDTH ** -0.5),
        "w_ssm_proj": nrm(ks[12], (DEPTH, SSM_INNER, D_MODEL), SSM_INNER ** -0.5),
        "w_out": nrm(ks[13], (DEPTH, D_MODEL, D_MODEL), D_MODEL ** -0.5),
        "norm_mix_post_w": gain(ks[14], D_MODEL),
        "norm_ffn_pre_w": gain(ks[15], D_MODEL),
        "w_up": nrm(ks[16], (DEPTH, D_MODEL, FFN_HIDDEN), D_MODEL ** -0.5),
        "w_down": nrm(ks[17], (DEPTH, FFN_HIDDEN, D_MODEL), FFN_HIDDEN ** -0.5),
        "norm_ffn_post_w": gain(ks[18], D_MODEL),
    }

def second_block(x, norm_mix_pre_w, w_in, b_gate, conv_w, conv_b, dt_bias, a_log, d_skip,
              ssm_norm_w, w_att_proj, w_ssm_proj, w_out, norm_mix_post_w, norm_ffn_pre_w,
              w_up, w_down, norm_ffn_post_w):
    b, s, _ = x.shape
    slopes = alibi_slopes(N_ATT_HEADS)
    offsets = [int(o) for o in np.cumsum(IN_SPLITS_2)[:-1]]
    h = x
    for layer in range(DEPTH):
        u = rmsnorm(h, norm_mix_pre_w[layer])
        proj = u @ w_in[layer]
        q, k, v, z, xbc, dt_raw, gate_logits = jnp.split(proj, offsets, axis=-1)
        q = q.reshape(b, s, N_ATT_HEADS, HEAD_DIM)
        k = k.reshape(b, s, N_ATT_HEADS, HEAD_DIM)
        v = v.reshape(b, s, N_ATT_HEADS, HEAD_DIM)
        outs, maxes, dens = [], [], []
        for window, dilation in DILATED_PATTERNS:
            o_g, m_g, l_g = dilated_window_attention(q, k, v, slopes, window, dilation)
            outs.append(o_g)
            maxes.append(m_g)
            dens.append(l_g)
        m_all = jnp.stack(maxes)
        wts = jnp.exp(m_all - jnp.max(m_all, axis=0, keepdims=True)) * jnp.stack(dens)
        att = jnp.sum(wts[..., None] * jnp.stack(outs), axis=0) / jnp.sum(wts, axis=0)[..., None]
        att = att.reshape(b, s, ATT_WIDTH).astype(x.dtype) @ w_att_proj[layer]
        ssm = mamba2_mixer(z, xbc, dt_raw, conv_w[layer], conv_b[layer], dt_bias[layer],
                           a_log[layer], d_skip[layer], ssm_norm_w[layer])
        ssm = ssm @ w_ssm_proj[layer]
        gates = jax.nn.sigmoid(gate_logits + b_gate[layer])
        g_att, g_ssm = jnp.split(gates, 2, axis=-1)
        mixed = (g_att * att + g_ssm * ssm) @ w_out[layer]
        h = h + rmsnorm(mixed, norm_mix_post_w[layer])
        f = rmsnorm(h, norm_ffn_pre_w[layer])
        f = jnp.square(jax.nn.relu(f @ w_up[layer])) @ w_down[layer]
        h = h + rmsnorm(f, norm_ffn_post_w[layer])
    return h


def setup_inputs(seed=0):
    out = dict(first_inputs(seed))
    for name, value in second_inputs(seed + 1).items():
        if name != "x":
            out[name + "_2"] = value
    return out


def reference(
    x, mem, g_mix, w_in, b_if, b_gate, conv_w, conv_b, ml_norm_g, g_mem, w_mem_kv, q_norm_g,
    k_norm_g, w_sb_proj, w_ml_proj, w_x_proj, w_out, g_mlp, w_ff1, w_ff2, norm_mix_pre_w_2,
    w_in_2, b_gate_2, conv_w_2, conv_b_2, dt_bias_2, a_log_2, d_skip_2, ssm_norm_w_2,
    w_att_proj_2, w_ssm_proj_2, w_out_2, norm_mix_post_w_2, norm_ffn_pre_w_2, w_up_2, w_down_2,
    norm_ffn_post_w_2,
):
    x = first_block(
        x, mem, g_mix, w_in, b_if, b_gate, conv_w, conv_b, ml_norm_g, g_mem, w_mem_kv, q_norm_g,
        k_norm_g, w_sb_proj, w_ml_proj, w_x_proj, w_out, g_mlp, w_ff1, w_ff2,
    )
    return second_block(
        x, norm_mix_pre_w_2, w_in_2, b_gate_2, conv_w_2, conv_b_2, dt_bias_2, a_log_2, d_skip_2,
        ssm_norm_w_2, w_att_proj_2, w_ssm_proj_2, w_out_2, norm_mix_post_w_2, norm_ffn_pre_w_2,
        w_up_2, w_down_2, norm_ffn_post_w_2,
    )


_drawn_inputs = setup_inputs


def setup_inputs(seed=0):
    import zlib

    import numpy as np

    out = dict(_drawn_inputs(seed))
    spreads = {}
    factors = {'g_mix': 3.634,
     'b_gate': 8.0,
     'conv_b': 64.0,
     'ml_norm_g': 40.872,
     'g_mem': 8.0,
     'q_norm_g': 8.0,
     'k_norm_g': 8.0,
     'g_mlp': 8.453,
     'b_gate_2': 200.0,
     'conv_b_2': 200.0,
     'norm_mix_pre_w_2': 8.0,
     'dt_bias_2': 3.97,
     'd_skip_2': 64.0,
     'ssm_norm_w_2': 64.0,
     'norm_mix_post_w_2': 64.0,
     'norm_ffn_pre_w_2': 64.0,
     'norm_ffn_post_w_2': 64.0,
     'a_log_2': 3.349}
    for name, (base, spread) in spreads.items():
        noise = np.random.default_rng([zlib.crc32(name.encode()), seed]).standard_normal(out[name].shape)
        drawn = base * np.exp(spread * noise) if base else spread * noise
        out[name] = jnp.asarray(drawn.astype(out[name].dtype))
    for name, factor in factors.items():
        out[name] = (out[name] * factor).astype(out[name].dtype)
    return out
```

```python
import concourse.bass as bass
from concourse import mybir
from contextlib import ExitStack

FP32 = mybir.dt.float32
FP32R = mybir.dt.float32r
ALU = mybir.AluOpType
ACT = mybir.ActivationFunctionType
AXX = mybir.AxisListType.X

P = 128
T = 256
D = 1024
KT = D // P
CW = 256
EPS = 1e-6
SLOTS = 3

SBQ, SBK, SBV, MLQ, MLK, MLV, MLO, MLI = (n * D for n in range(8))
XQ = MLI + 8
GATE = XQ + D
AQ, AK, AV = 0, 768, 1536
SZ = 2304
SX = SZ + 2048
SB_ = SX + 2048
SC = SB_ + 1024
SDT = SC + 1024
GATE2 = SDT + 32

H0, M0, Y0 = 0, 8, 16
YSB, YML, YX = Y0, Y0 + 8, Y0 + 16
YAT, YSS = Y0, Y0 + 6
U0 = 8
OPND = 40

PARAM_TILES = (
    (("conv_w_2", 128),),
    (("conv_w", 64), ("conv_b", 16), ("g_mix", 8), ("g_mem", 8), ("g_mlp", 8), ("ml_norm_g", 8),
     ("q_norm_g", 2), ("k_norm_g", 2), ("norm_mix_pre_w_2", 8)),
    (("b_gate", 24), ("conv_b_2", 32), ("ssm_norm_w_2", 16), ("b_gate_2", 16), ("norm_mix_post_w_2", 8),
     ("norm_ffn_pre_w_2", 8), ("norm_ffn_post_w_2", 8)),
)


def param_columns():
    col = {}
    for t, tile in enumerate(PARAM_TILES):
        at = 0
        for name, rows in tile:
            col[name] = t * P + at
            at += rows
    return col


class Slots:

    def __init__(self):
        self.units, self.fills = [0] * SLOTS, [0] * SLOTS
        self.unit_step, self.fill_step = [0] * SLOTS, [0] * SLOTS
        self.trip = 0

    def enter(self, pattern, trip, filled=None):
        filled = pattern if filled is None else filled
        self.unit_step = [pattern.count(s) for s in range(SLOTS)]
        self.fill_step = [filled.count(s) for s in range(SLOTS)]
        self.trip = trip

    def leave(self, trips):
        for s in range(SLOTS):
            self.units[s] += self.unit_step[s] * (trips - 1)
            self.fills[s] += self.fill_step[s] * (trips - 1)
        self.unit_step, self.fill_step = [0] * SLOTS, [0] * SLOTS

    def take(self, s, fills=True):
        n = self.units[s] + (self.trip * self.unit_step[s] if self.unit_step[s] else 0)
        self.units[s] += 1
        self.fills[s] += fills
        return n

    def banks(self, s):
        return self.fills[s] + (self.trip * self.fill_step[s] if self.fill_step[s] else 0)


class Chain:

    def __init__(self, eng, sem):
        self.eng, self.sem, self.n, self.per, self.trip = eng, sem, 0, 0, 0

    def __call__(self, instruction):
        instruction.then_inc(self.sem, 1)
        self.n += 1
        self.eng.wait_ge(self.sem, self.n + (self.trip * self.per if self.per else 0))

    def enter(self, trip, per):
        self.trip, self.per, self.start = trip, per, self.n

    def leave(self, trips):
        assert self.n - self.start == self.per, (self.n - self.start, self.per)
        self.n += self.per * (trips - 1)
        self.per = 0


def build(nc, a, out):
    ctx = ExitStack()
    with ctx:
        def sb(name, shape, dt=FP32):
            return ctx.enter_context(nc.sbuf_tensor(name, shape, dt))

        sems = {}

        def S(name):
            if name not in sems:
                sems[name] = ctx.enter_context(nc.semaphore(name))
            return sems[name]

        raw = sb("raw", [P, SLOTS, KT, CW])
        w_hi = sb("w_hi", [P, SLOTS, KT, CW], FP32R)
        w_lo = sb("w_lo", [P, SLOTS, KT, CW], FP32R)
        x_hi = sb("x_hi", [P, OPND, T], FP32R)
        x_lo = sb("x_lo", [P, OPND, T], FP32R)
        res = sb("res", [P, KT, T])
        mix = sb("mix", [P, KT, T])
        cst = sb("cst", [P, 3 * P + 2 * 384])
        ident, ones, later = (cst[:, n * P:(n + 1) * P] for n in range(3))
        strict3 = cst[:, 3 * P:3 * P + 384]
        incl3 = cst[:, 3 * P + 384:]
        pcol = sb("pcol", [P, 3 * P])
        small = sb("small", [P, 1024])
        arena = sb("arena", [P, 7600])
        ps = ctx.enter_context(nc.psum_tensor("ps", [P, 8, 512], FP32))
        col = param_columns()

        def cells(at, *dims):
            n = 1
            for d in dims:
                n *= d
            v = arena[:, at:at + n]
            if len(dims) == 2:
                return v.rearrange("p (a b) -> p a b", a=dims[0])
            if len(dims) == 3:
                return v.rearrange("p (a b c) -> p a b c", a=dims[0], b=dims[1])
            return v

        def bank(b, *dims):
            v = ps[:, b, :]
            if len(dims) == 2:
                return v[:, 0:dims[0] * dims[1]].rearrange("p (a b) -> p a b", a=dims[0])
            return v[:, 0:dims[0]]

        def pc(name, k=0):
            if isinstance(k, int):
                return pcol[:, col[name] + k:col[name] + k + 1]
            return pcol[:, bass.ds(k + col[name], 1)]

        def rows(t, at, n):
            return t[:, at:at + n, :] if isinstance(at, int) else t[:, bass.ds(at, n), :]

        def need(eng, name, n):
            if not isinstance(n, int) or n > 0:
                eng.wait_ge(S(name), n)

        eps = small[:, 0:1]
        bif = small[:, 8:16]
        wif = small[:, 16:80].rearrange("p (k c) -> p k c", k=KT)
        gz = small[:, 80:96].rearrange("p (t c) -> p t c", t=2)
        acol = small[:, 96:104].rearrange("p (t h) -> p t h", t=2)
        gt1 = small[:, 104:120].rearrange("p (t c) -> p t c", t=2)
        cx = small[:, 128:144]
        ssq = small[:, 144:160]
        wdt = small[:, 256:512].rearrange("p (k c) -> p k c", k=KT)
        dtb, neg_a = small[:, 512:544], small[:, 544:576]
        dtz, dtc, la, nacs = (small[:, n:n + 64].rearrange("p (t h) -> p t h", t=2) for n in (576, 640, 704, 768))
        skip = small[:, 832:848]
        ax = small[:, 848:880]

        w_in, w_in2 = a["w_in"][0], a["w_in_2"][0]

        def cols_of(w, k0, nk, at, n=CW):
            c = slice(at, at + n) if isinstance(at, int) else bass.ds(at, n)
            return w[k0 * P:(k0 + nk) * P, c].rearrange("(k p) n -> p k n", p=P)

        def load(eng, sl, s, parts):
            n = sl.take(s)
            need(eng, f"w_split{s}", n)
            for src, k0, nk, c0, nc_ in parts:
                eng.dma_start(raw[:, s, k0:k0 + nk, c0:c0 + nc_], src).then_inc(S(f"w_in{s}"), 16)

        def halves(w, k0, at, nk=KT):
            h = nk // 2
            return [(cols_of(w, k0 + n, h, at), n, h, 0, CW) for n in (h, 0)]

        def split_hi(act, sl, s):
            n = sl.take(s)
            act.wait_ge(S(f"w_in{s}"), n * 32 + 32)
            need(act, f"unit{s}", n)
            nc.scalar.copy(w_hi[:, s], raw[:, s]).then_inc(S(f"w_hi{s}"), 1)

        def split_lo(dve, sl, s):
            n = sl.take(s)
            dve.wait_ge(S(f"w_hi{s}"), n + 1)
            nc.vector.tensor_tensor(w_lo[:, s], raw[:, s], w_hi[:, s].bitcast(FP32), ALU.subtract)\
                .then_inc(S(f"w_split{s}"), 1)

        def products(pe, s, o, at, tok, nk=KT, out_=None, start=True, stop=True):
            dst = bank(s, 2, CW)[:, o] if out_ is None else out_
            for k in range(nk):
                for m, (wt, xt) in enumerate(((w_hi, x_hi), (w_hi, x_lo), (w_lo, x_hi))):
                    if tok:
                        l, r = xt[:, at + k, o * P:(o + 1) * P], wt[:, s, k, :]
                    else:
                        l, r = wt[:, s, k, o * P:(o + 1) * P], xt[:, at + k, :]
                    last = nc.tensor.matmul(dst, l, r, start=start and k == 0 and m == 0,
                                            stop=stop and k == nk - 1 and m == 2)
            return last

        def begin(pe, sl, s):
            need(pe, f"bank{s}", sl.banks(s))
            pe.wait_ge(S(f"w_split{s}"), sl.take(s) + 1)

        block = ctx.enter_context(nc.Block())

        @block.sync
        def _(sp):
            sl = Slots()
            xtok, mtok = cells(0, 2, D), cells(2048, 2, D)
            sp.dma_start(xtok, a["x"][0].rearrange("(t p) d -> p t d", p=P)).then_inc(S("x_in"), 16)
            sp.dma_start(mtok, a["mem"][0].rearrange("(t p) d -> p t d", p=P)).then_inc(S("m_in"), 16)

            def at(v):
                return v if isinstance(v, int) else sp.snap(v)

            def cross(i):
                yield 0, halves(a["w_mem_kv"][0], 0, at(i * CW))
                yield 1, halves(w_in, 0, at(i * CW + XQ))
                yield 2, halves(a["w_mem_kv"][0], 0, at(i * CW + D))

            def stick(i):
                for s, c in enumerate((SBQ, SBK, SBV)):
                    yield s, halves(w_in, 0, at(i * CW + c))

            def mlstm(i):
                for s, c in zip((0, 1, 2, 1), (MLQ, MLK, MLV, MLO)):
                    yield s, halves(w_in, 0, at(i * CW + c))

            def gated(w, wp, gate):
                def units(i):
                    yield 0, halves(w, 0, at(i * CW + gate))
                    yield 1, halves(wp, 0, at(i * CW))
                return units

            def plain(w, n):
                def units(i):
                    for b in range(n):
                        yield (0, 1, 2, 1)[b] if n == 4 else b, halves(w, 0, at((i * n + b) * CW))
                return units

            def deep(w, kb):
                def units(i):
                    for b in range(2 * kb):
                        yield (0, 1, 2, 1)[b % 4], halves(w, b % kb * KT, at((i * 2 + b // kb) * CW))
                return units

            def run(units, trips, pattern):
                sl.enter(pattern, 0)
                with sp.Fori(0, trips) as i:
                    sl.trip = i
                    for s, parts in units(i):
                        load(sp, sl, s, parts)
                sl.leave(trips)

            for s, parts in cross(0):
                load(sp, sl, s, parts)
            run(lambda i: cross(i + 1), 3, (0, 1, 2))
            run(stick, 4, (0, 1, 2))
            run(mlstm, 4, (0, 1, 2, 1))
            for w, g in (("w_x_proj", 2), ("w_sb_proj", 0), ("w_ml_proj", 1)):
                run(gated(w_in, a[w][0], GATE + g * D), 4, (0, 1))
            for s, parts in plain(a["w_out"][0], 4)(0):
                load(sp, sl, s, parts)
            run(plain(a["w_ff1"][0], 4), 4, (0, 1, 2, 1))
            run(deep(a["w_ff2"][0], 4), 2, (0, 1, 2, 1) * 2)

            def att(i):
                for s, c in enumerate((AQ, AK, AV)):
                    yield s, halves(w_in2, 0, at(i * CW + c))

            def ssm(i):
                yield 0, halves(w_in2, 0, at(i * CW + SX))
                yield 1, [(cols_of(w_in2, 0, KT, at(i * P + c), P), 0, KT, n * P, P)
                          for n, c in enumerate((SB_, SC))]
                yield 2, halves(w_in2, 0, at(i * CW + SZ))

            def gated_att(i):
                yield 0, halves(w_in2, 0, at(i * CW + GATE2))
                yield 1, halves(a["w_att_proj_2"][0], 0, at(i * CW), 6)

            def gated_ssm(i):
                yield 0, halves(w_in2, 0, at(i * CW + GATE2 + D))
                yield 1, halves(a["w_ssm_proj_2"][0], 0, at(i * CW))
                yield 2, halves(a["w_ssm_proj_2"][0], KT, at(i * CW))

            run(att, 3, (0, 1, 2))
            run(ssm, 8, (0, 1, 2))
            run(gated_att, 4, (0, 1))
            run(gated_ssm, 4, (0, 1, 2))
            for s, parts in plain(a["w_out_2"][0], 4)(0):
                load(sp, sl, s, parts)
            run(plain(a["w_up_2"][0], 4), 4, (0, 1, 2, 1))
            run(deep(a["w_down_2"][0], 4), 2, (0, 1, 2, 1) * 2)
            sp.wait_ge(S("y_ready"), 1)
            sp.dma_start(out[0].rearrange("(t p) d -> p t d", p=P), cells(0, 2, D)).then_inc(S("y_out"), 16)
            sp.wait_ge(S("y_out"), 16)

        @block.gpsimd
        def _(pool):
            nc.gpsimd.memset(cells(4096, 3, P), 0.0).then_inc(S("prow0"), 1)
            nc.gpsimd.memset(eps, EPS).then_inc(S("prow0"), 1)
            pool.dma_start(bif, a["b_if"].partition_broadcast(P)).then_inc(S("gate_in"), 16)
            pool.dma_start(wif, w_in[:, MLI:MLI + 8].rearrange("(k p) n -> p k n", p=P))\
                .then_inc(S("gate_in"), 16)

            pool.dma_start(wdt, w_in2[:, SDT:SDT + 32].rearrange("(k p) n -> p k n", p=P)).then_inc(S("dt_in"), 16)
            pool.dma_start(dtb, a["dt_bias_2"].partition_broadcast(P)).then_inc(S("dt_in"), 16)
            pool.dma_start(neg_a, a["a_log_2"].partition_broadcast(P)).then_inc(S("dt_in"), 16)
            for o in range(2):
                with nc.allow_non_contiguous_dma(reason="thirty-two scalars"):
                    pool.dma_start(skip[64 * o:64 * o + 64, :],
                                   a["d_skip_2"].rearrange("l (k o) -> l o k", o=2)[:, o, :].partition_broadcast(64))\
                        .then_inc(S("dt_in"), 16)

            pool.wait_ge(S("g_rows"), 1)
            pool.dma_start(a["rows"][0:2, 0:4].rearrange("r h t -> h r t"), cells(5120, 2, T)[0:4])\
                .then_inc(S("g_out"), 16)
            pool.wait_ge(S("g_out"), 16)

            def ml_rows(j):
                need(pool, "m_hm", j)
                pool.dma_start(cells(4112, 2, T), ml_src(j)).then_inc(S("m_bc"), 16)

            def ml_src(j):
                r = a["rows"][0:2, j:j + 1, :] if isinstance(j, int) else a["rows"][0:2, bass.ds(j, 1), :]
                return r.rearrange("r h t -> (r h) t").partition_broadcast(P)

            pool.wait_ge(S("s_lo"), 4)
            ml_rows(0)
            with pool.Fori(0, 3) as j:
                ml_rows(j + 1)

            def att_bias(j):
                need(pool, "a_b", j)
                h = slice(4 * j, 4 * j + 4) if isinstance(j, int) else bass.ds(4 * j, 4)
                pool.dma_start(cells(1536, 4, 384), a["att_bias"][:, h, :]).then_inc(S("a_bias"), 16)

            pool.wait_ge(S("dt_rows"), 1)
            pool.dma_start(a["rows"][2], cells(5120, T)[0:32]).then_inc(S("dt_out"), 16)
            pool.wait_ge(S("dt_out"), 16)
            pool.wait_ge(S("dt_col"), 1)
            att_bias(0)
            with pool.Fori(0, 2) as j:
                att_bias(j + 1)

            def decay_rows(j):
                need(pool, "d_d", j)
                h = slice(4 * j, 4 * j + 4) if isinstance(j, int) else bass.ds(4 * j, 4)
                pool.dma_start(cells(3600, 4, T), a["rows"][2, h, :].partition_broadcast(P)).then_inc(S("d_bc"), 16)

            pool.wait_ge(S("a_lo"), 3)
            decay_rows(0)
            with pool.Fori(0, 7) as j:
                decay_rows(j + 1)


        @block.scalar
        def _(act):
            sl, ev = Slots(), Slots()
            chain = Chain(act, S("act_chain"))
            A = nc.scalar.activation

            def inv_rms(dst, src, n):
                chain(A(dst, src, ACT.Ln, bias=eps, scale=1.0 / n))
                return A(dst, dst, ACT.Exp, scale=-0.5)

            def tables():
                act.preload_act_table_set("natural_log_exp_and_others")

            def evac(s, dst, func=ACT.Copy):
                act.wait_ge(S(f"unit{s}"), ev.take(s) + 1)
                A(dst, bank(s, 2, CW), func).then_inc(S(f"bank{s}"), 1)

            def split(s):
                split_hi(act, sl, s)

            def phase(body, trips, pattern, chained):
                body(0, None)
                sl.enter(pattern, 0)
                ev.enter(pattern, 0)
                with act.Fori(0, trips - 1) as j:
                    sl.trip = ev.trip = j
                    chain.enter(j, chained)
                    body(j + 1, j)
                sl.leave(trips - 1)
                ev.leave(trips - 1)
                chain.leave(trips - 1)
                body(None, trips - 1)

            def loop(body, trips, pattern, chained=0, filled=None):
                sl.enter(pattern, 0)
                ev.enter(pattern, 0, filled)
                with act.Fori(0, trips) as i:
                    sl.trip = ev.trip = i
                    chain.enter(i, chained)
                    body(i)
                sl.leave(trips)
                ev.leave(trips)
                chain.leave(trips)

            act.dma_start(cst[:, :], a["consts"]).then_inc(S("cst_in"), 16)
            prow = cells(4096, 3, P)
            act.wait_ge(S("prow0"), 2)
            for t, tile in enumerate(PARAM_TILES):
                at = 0
                for name, n in tile:
                    v = a[name][0]
                    v = v.rearrange("j (r c) -> (j r) c", c=P) if len(v.shape) == 2 else \
                        v.rearrange("(r c) -> r c", c=P)
                    act.dma_start(prow[at:at + n, t, :], v).then_inc(S("prow_in"), 16)
                    at += n
            tables()
            act.wait_ge(S("prow0"), 2)
            xtok, mtok = cells(0, 2, D), cells(2048, 2, D)
            junk = mix[:, :, :].rearrange("p (t c) n -> p t (c n)", t=2)
            for n, src in enumerate((xtok, mtok)):
                act.wait_ge(S(("x_in", "m_in")[n]), 16)
                for t in range(2):
                    last = A(junk[:, t], src[:, t], ACT.Square, accum_out=ssq[:, 2 * n + t:2 * n + t + 1])
                chain(last)
                inv_rms(ssq[:, 2 * n:2 * n + 2], ssq[:, 2 * n:2 * n + 2], D).then_inc(S("x_rs"), 1)
            split(0)
            act.wait_ge(S("pcol"), 1)
            for n, g in enumerate(("g_mix", "g_mem")):
                if n == 1:
                    split(1)
                for b in range(4):
                    act.wait_ge(S("h_t"), 4 * n + b + 1)
                    for k in range(2):
                        last = A(x_hi[:, (H0, M0)[n] + 2 * b + k], bank(b, 2, T)[:, k], ACT.Identity,
                                 scale=pc(g, 2 * b + k))
                    last.then_inc(S("h_hi"), 1)
            act.wait_ge(S("g_b"), 1)
            lf = gt1[:, :, 4:8]
            chain(A(lf, gz[:, :, 4:8], ACT.Abs))
            chain(A(lf, lf, ACT.Exp, scale=-1.0))
            A(lf, lf, ACT.Ln, bias=1.0).then_inc(S("g_sp"), 1)

            kq, cv_, csq, cr, cp = (cells(0, 4, T), cells(1024, 2, T), cells(1536, 4, T), cells(2560, 2, T),
                                    cells(4096, 2, T))

            def cross(i, j):
                kb, qb = ev.banks(0), ev.banks(1)
                if j is not None:
                    need(act, "bank0", kb)
                    need(act, "bank1", qb)
                    A(csq, kq, ACT.Square).then_inc(S("c_sq"), 1)
                if i is not None:
                    split(2)
                if j is not None:
                    act.wait_ge(S("c_ss"), j + 1)
                    inv_rms(cr, bank(3, 2, T), T).then_inc(S("c_r"), 1)
                if i is not None:
                    split(0)
                if j is not None:
                    act.wait_ge(S("c_mx"), j + 1)
                    for t in range(2):
                        last = A(cp[:, t], bank(4, 2, T)[:, t], ACT.Exp, bias=cx[:, t:t + 1], scale=1.0 / 16,
                                 accum_out=cx[:, 2 + t:3 + t])
                    last.then_inc(S("c_p"), 1)
                if i is not None:
                    split(1)
                if j is not None:
                    act.wait_ge(S("c_y"), j + 1)
                    A(rows(x_hi, 2 * j + YX, 2), bank(6, 2, T), ACT.Copy).then_inc(S("c_hi"), 1)
                if i is not None:
                    ev.take(0)
                    ev.take(1)
                    evac(2, cv_)

            act.wait_ge(S("res"), 4)
            phase(cross, 4, (0, 1, 2), 1)

            sv_, se, sp_, sls = cells(1024, 2, T), cells(1536, 2, 384), cells(2304, 2, 384), cells(3840, 2, 384)

            def stick(i, j):
                if i is not None:
                    split(2)
                if j is not None:
                    act.wait_ge(S("s_z"), j + 1)
                    A(se, ps[:, 3:5, 0:384], ACT.Abs, scale=P ** -0.5).then_inc(S("s_abs"), 1)
                    act.wait_ge(S("s_abs"), j + 1)
                    chain(A(se, se, ACT.Exp, scale=-1.0))
                    A(sp_, se, ACT.Ln, bias=1.0).then_inc(S("s_sp"), 1)
                if i is not None:
                    split(0)
                if j is not None:
                    act.wait_ge(S("s_la"), j + 1)
                    A(sp_, sls, ACT.Exp).then_inc(S("s_A"), 1)
                if i is not None:
                    split(1)
                if j is not None:
                    act.wait_ge(S("s_y"), j + 1)
                    A(rows(x_hi, 2 * j + YSB, 2), bank(7, 2, T), ACT.Copy).then_inc(S("s_hi"), 1)
                if i is not None:
                    ev.take(0)
                    ev.take(1)
                    evac(2, sv_)

            phase(stick, 4, (0, 1, 2), 1)

            qkp, cv, sg, mv, mo = (cells(0, 4, 260), cells(1040, 4, T), cells(2064, 4, T), cells(3088, 2, T),
                                   cells(3600, 2, T))
            mbc, w_, me, mhm, msq, mr = (cells(4112, 2, T), cells(4624, 384), cells(5392, T), cells(5648, 2, T),
                                         cells(6160, 2, T), cells(6672, T))
            act.wait_ge(S("s_lo"), 4)

            def mlstm(i, j):
                gates = ev.banks(1)
                if i is not None:
                    split(2)
                if j is not None:
                    act.wait_ge(S("m_w0"), j + 1)
                    A(w_, w_, ACT.Exp).then_inc(S("m_w"), 1)
                    A(me, mbc[:, 1], ACT.Exp).then_inc(S("m_e"), 1)
                if i is not None:
                    evac(0, qkp[:, 0:2, 3:259])
                    split(1)
                    ev.take(1)
                    split(0)
                if j is not None:
                    act.wait_ge(S("m_den"), j + 1)
                    A(mr, bank(4, T), ACT.Abs).then_inc(S("m_abs"), 1)
                if i is not None:
                    act.wait_ge(S("m_cv"), i + 1)
                    A(sg, cv, ACT.Sigmoid).then_inc(S("m_sg"), 1)
                if j is not None:
                    need(act, "bank1", gates)
                    A(mo, mo, ACT.Sigmoid).then_inc(S("m_o"), 1)
                    tables()
                    act.wait_ge(S("m_hm"), j + 1)
                    A(msq, mhm, ACT.Square).then_inc(S("m_sq"), 1)
                if i is not None:
                    evac(2, mv)
                    split(1)
                if j is not None:
                    act.wait_ge(S("m_ss"), j + 1)
                    inv_rms(mr, bank(6, T), T).then_inc(S("m_r"), 1)
                    act.wait_ge(S("m_y"), j + 1)
                    A(rows(x_hi, 2 * j + YML, 2), mhm, ACT.Copy).then_inc(S("m_hi"), 1)
                elif i is not None:
                    tables()
                if i is not None:
                    evac(1, mo)

            phase(mlstm, 4, (0, 1, 2, 1), 1)

            gt = cells(0, 2, T)

            def gated(bias, first, last_, proj=(1,), b_gate="b_gate"):
                def body(i):
                    if len(proj) == 1:
                        split(0)
                    act.wait_ge(S("unit0"), ev.take(0) + 1)
                    act.wait_ge(S("p_used"), i + first + 1)
                    for c in range(2):
                        last = A(gt[:, c], bank(0, 2, CW)[:, c], ACT.Sigmoid, bias=pc(b_gate, 2 * i + bias + c))
                    last.then_inc(S("bank0"), 1)
                    if len(proj) == 1:
                        split(1)
                        ev.take(1)
                    else:
                        for s in (2, 0, 1):
                            split(s)
                        for s in proj:
                            ev.take(s, False)
                    if last_:
                        act.wait_ge(S("p_used"), i + first + 2)
                        A(rows(x_hi, 2 * i + M0, 2), rows(mix, 2 * i, 2), ACT.Copy).then_inc(S("mix_hi"), 1)
                return body

            act.wait_ge(S("m_lo"), 4)
            for n, g in enumerate((2, 0, 1)):
                loop(gated(8 * g, 4 * n, n == 2), 4, (0, 1))
            tables()

            def norm(n, src, g=None, at=0):
                sqs, t, r = cells(0, KT, T), cells(2048, KT, T), cells(4096, T)
                for k in range(KT):
                    A(sqs[:, k], src[:, k], ACT.Square).then_inc(S("n_sq"), 1)
                act.wait_ge(S("n_ss"), n + 1)
                inv_rms(r, bank(3, T), D).then_inc(S("n_r"), 1)
                if g is None:
                    return
                for k in range(KT):
                    act.wait_ge(S("n_t"), 4 * n + k // 2 + 1)
                    A(x_hi[:, at + k], t[:, k], ACT.Identity, scale=pc(g, k)).then_inc(S("n_hi"), 1)

            def four_taken():
                for s in (0, 1, 2, 1):
                    ev.take(s)
                for s in (2, 1, 0, 1):
                    split(s)
                for s in range(SLOTS):
                    act.wait_ge(S(f"bank{s}"), ev.banks(s))

            four_taken()
            norm(0, res, "g_mlp", H0)

            def hidden(c0):
                def body(i):
                    for b, s in enumerate((0, 1, 2, 1)):
                        act.wait_ge(S(f"unit{s}"), ev.take(s) + 1)
                        c = 4 * i + b
                        f = cells(512 * (b % 2), 2, T)
                        A(f, bank(s, 2, CW), ACT.Relu).then_inc(S(f"bank{s}"), 1)
                        split((2, 1, 0, 1)[b])
                        act.wait_ge(S("f_sq"), c + c0 + 1)
                        A(rows(x_hi, 2 * c + U0, 2), cells(1024 + 512 * (b % 2), 2, T), ACT.Copy)\
                            .then_inc(S("f_hi"), 1)
                return body

            loop(hidden(0), 4, (0, 1, 2, 1))

            def deep(n):
                def body(i):
                    for b in range(n):
                        ev.take((0, 1, 2, 1)[b % 4], False)
                        split((2, 1, 0, 1)[b % 4])
                return body

            loop(deep(8), 2, (0, 1, 2, 1) * 2, filled=())

            act.wait_ge(S("deep1"), 3)
            norm(1, res, "norm_mix_pre_w_2", H0)
            act.wait_ge(S("dt_in"), 80)
            A(neg_a, neg_a, ACT.Exp).then_inc(S("dt_a"), 1)
            act.wait_ge(S("dt_b"), 1)
            chain(A(la, dtz, ACT.Abs))
            chain(A(la, la, ACT.Exp, scale=-1.0))
            A(la, la, ACT.Ln, bias=1.0).then_inc(S("dt_sp"), 1)

            av, ap_, apT = cells(1024, 2, T), cells(3072, 4, 384), cells(4608, 4, 384)

            def att(i, j):
                if i is not None:
                    split(2)
                    split(0)
                if j is not None:
                    act.wait_ge(S("a_mx"), j + 1)
                    for h in range(4):
                        for t, v in enumerate((slice(0, P), slice(P, 384))):
                            last = A(ap_[:, h, v], ap_[:, h, v], ACT.Exp, bias=ax[:, 4 * t + h:4 * t + h + 1],
                                     accum_out=ax[:, 8 + 4 * t + h:9 + 4 * t + h])
                    last.then_inc(S("a_p"), 1)
                if i is not None:
                    split(1)
                if j is not None:
                    act.wait_ge(S("a_t"), j + 1)
                    A(apT, ps[:, 3:7, 0:384], ACT.Copy).then_inc(S("a_pt"), 1)
                    act.wait_ge(S("a_y"), j + 1)
                    A(rows(x_hi, 2 * j + YAT, 2), bank(7, 2, T), ACT.Copy).then_inc(S("a_hi"), 1)
                if i is not None:
                    ev.take(0)
                    ev.take(1)
                    evac(2, av)

            phase(att, 3, (0, 1, 2), 0)

            dxp, dcv, dsg, dz = cells(0, 4, 260), cells(1040, 4, T), cells(2064, 4, T), cells(3088, 2, T)
            dec, dsq, dr, dy = cells(5520, 4, 384), cells(5520, 2, T), cells(4624, T), cells(7056, 2, T)
            act.wait_ge(S("a_lo"), 3)

            def ssm(i, j):
                if i is not None:
                    split(2)
                if j is not None:
                    act.wait_ge(S("d_d"), j + 1)
                    A(dec, dec, ACT.Exp).then_inc(S("d_e"), 1)
                if i is not None:
                    evac(0, dxp[:, 0:2, 3:259])
                    split(0)
                    ev.take(1)
                    split(1)
                if j is not None:
                    act.wait_ge(S("d_y"), j + 1)
                    A(dsq, dy, ACT.Square).then_inc(S("d_sq"), 1)
                if i is not None:
                    act.wait_ge(S("d_cv"), i + 1)
                    A(dsg, dcv, ACT.Sigmoid).then_inc(S("d_sg"), 1)
                    act.wait_ge(S("unit2"), ev.take(2) + 1)
                    A(dz, bank(2, 2, CW), ACT.Sigmoid).then_inc(S("d_zs"), 1)
                    tables()
                if j is not None:
                    act.wait_ge(S("d_ss"), j + 1)
                    inv_rms(dr, bank(6, T), T).then_inc(S("d_r"), 1)
                    act.wait_ge(S("d_yn"), j + 1)
                    A(rows(x_hi, 2 * j + YSS, 2), dy, ACT.Copy).then_inc(S("d_hi"), 1)

            phase(ssm, 8, (0, 1, 2), 1)
            act.wait_ge(S("d_lo"), 8)
            loop(gated(0, 12, False, b_gate="b_gate_2"), 4, (0, 1))
            loop(gated(8, 16, True, (1, 2), "b_gate_2"), 4, (0, 1, 2), 0, (0,))
            tables()
            four_taken()
            norm(2, mix)
            act.wait_ge(S("r_post"), 1)
            norm(3, res, "norm_ffn_pre_w_2", H0)
            loop(hidden(16), 4, (0, 1, 2, 1))
            for i in range(2):
                for b in range(8):
                    if i == 0 or b < 6:
                        split((2, 1, 0, 1)[b % 4])
            act.wait_ge(S("deep1"), 5)
            norm(4, mix)

        @block.vector
        def _(dve):
            sl, ev = Slots(), Slots()
            chain = Chain(dve, S("dve_chain"))
            V = nc.vector
            tt, ts, stt = V.tensor_tensor, V.tensor_scalar, V.scalar_tensor_tensor

            def split(s):
                split_lo(dve, sl, s)

            def evac(s, dst):
                dve.wait_ge(S(f"unit{s}"), ev.take(s) + 1)
                V.tensor_copy(dst, bank(s, 2, CW)).then_inc(S(f"bank{s}"), 1)

            def phase(body, trips, pattern, chained):
                body(0, None)
                sl.enter(pattern, 0)
                ev.enter(pattern, 0)
                with dve.Fori(0, trips - 1) as j:
                    sl.trip = ev.trip = j
                    chain.enter(j, chained)
                    body(j + 1, j)
                sl.leave(trips - 1)
                ev.leave(trips - 1)
                chain.leave(trips - 1)
                body(None, trips - 1)

            def loop(body, trips, pattern, chained=0, filled=None):
                sl.enter(pattern, 0)
                ev.enter(pattern, 0, filled)
                with dve.Fori(0, trips) as i:
                    sl.trip = ev.trip = i
                    chain.enter(i, chained)
                    body(i)
                sl.leave(trips)
                ev.leave(trips)
                chain.leave(trips)

            def bc(v, n, at=1):
                v = v.unsqueeze(at)
                return v.broadcast_to([*v.shape[:at], n, *v.shape[at + 1:]])

            def low(at, src, hi_name, n, lo_name, k=2):
                dve.wait_ge(S(hi_name), n)
                tt(rows(x_lo, at, k), src, rows(x_hi, at, k).bitcast(FP32), ALU.subtract).then_inc(S(lo_name), 1)

            for n, name in enumerate(("p_used", "q_proj", "deep0", "deep1")):
                V.memset(small[:, 900 + n:901 + n], 0.0).then_inc(S(name), 1)
            dve.wait_ge(S("pcol_t"), 1)
            V.tensor_copy(pcol[:, :], bank(7, 384)).then_inc(S("pcol"), 1)
            xtok, mtok, xn = cells(0, 2, D), cells(2048, 2, D), cells(4480, 2, D)
            dve.wait_ge(S("x_rs"), 1)
            for t in range(2):
                last = ts(xn[:, t], xtok[:, t], ssq[:, t:t + 1], None, ALU.mult)
            last.then_inc(S("xn"), 1)
            dve.wait_ge(S("x_rs"), 2)
            for t in range(2):
                last = ts(mtok[:, t], mtok[:, t], ssq[:, 2 + t:3 + t], None, ALU.mult)
            last.then_inc(S("mn"), 1)
            dve.wait_ge(S("pcol"), 1)
            for n, g in enumerate(("g_mix", "g_mem")):
                for b in range(4):
                    dve.wait_ge(S("h_hi"), 4 * n + b + 1)
                    for k in range(2):
                        at = (H0, M0)[n] + 2 * b + k
                        last = stt(x_lo[:, at], bank(b, 2, T)[:, k], pc(g, 2 * b + k), x_hi[:, at].bitcast(FP32),
                                   ALU.mult, ALU.subtract)
                    last.then_inc(S("h_lo"), 1)
            split(0)
            split(1)
            for b in range(4):
                dve.wait_ge(S("res_t"), b + 1)
                V.tensor_copy(res[:, 2 * b:2 * b + 2], bank(b, 2, T)).then_inc(S("res"), 1)
            dve.wait_ge(S("gate_in"), 32)
            dve.wait_ge(S("g_z"), 1)
            tt(gz, bank(4, 2, 8), bc(bif, 2), ALU.add).then_inc(S("g_b"), 1)
            dve.wait_ge(S("g_sp"), 1)
            stt(gt1[:, :, 4:8], gz[:, :, 4:8], 0.0, gt1[:, :, 4:8], ALU.min, ALU.subtract)
            V.tensor_copy(gt1[:, :, 0:4], gz[:, :, 0:4]).then_inc(S("g_lf"), 1)
            one, bsum, top, arow = (cells(n, T)[0:4] for n in (6400, 5888, 6144, 5632))
            outr = cells(5120, 2, T)[0:4]
            dve.wait_ge(S("g_t"), 1)
            chain(V.memset(one, 1.0))
            chain(V.tensor_tensor_scan(bsum, one, bank(5, 2, T)[0:4, 1], 0.0, ALU.mult, ALU.add))
            chain(tt(arow, bank(5, 2, T)[0:4, 0], bsum, ALU.subtract))
            chain(V.tensor_tensor_scan(top, arow, arow, 0.0, ALU.max, ALU.max))
            ts(outr[:, 0], top, -1.0, None, ALU.mult)
            stt(outr[:, 1], bsum, -1.0, top, ALU.mult, ALU.subtract).then_inc(S("g_rows"), 1)
            dve.wait_ge(S("g_ct"), 1)
            V.tensor_copy(acol, bank(6, 2, 4)).then_inc(S("g_col"), 1)

            kq, cr, kqn, cp, cpT = (cells(0, 4, T), cells(2560, 2, T), cells(3072, 4, T), cells(4096, 2, T),
                                    cells(4608, 2, T))

            def cross(i, j):
                if i is not None:
                    split(2)
                if j is not None:
                    dve.wait_ge(S("c_r"), j + 1)
                    for n in range(4):
                        g = pc(("k_norm_g", "q_norm_g")[n // 2], n % 2)
                        last = stt(kqn[:, n], kq[:, n], g, cr[:, n // 2], ALU.mult, ALU.mult)
                    last.then_inc(S("c_n"), 1)
                    dve.wait_ge(S("c_n"), j + 1)
                if i is not None:
                    evac(0, kq[:, 0:2])
                    split(0)
                if j is not None:
                    dve.wait_ge(S("c_lg"), j + 1)
                    chain(V.tensor_reduce(cx[:, 4:6], bank(4, 2, T), AXX, ALU.max, negate=True))
                    ts(cx[:, 0:2], cx[:, 4:6], 1.0 / 16, None, ALU.mult).then_inc(S("c_mx"), 1)
                    dve.wait_ge(S("c_p"), j + 1)
                    chain(V.reciprocal(cx[:, 6:8], cx[:, 2:4]))
                    for t in range(2):
                        last = ts(cp[:, t], cp[:, t], cx[:, 6 + t:7 + t], None, ALU.mult)
                    last.then_inc(S("c_pn"), 1)
                    dve.wait_ge(S("c_t"), j + 1)
                    V.tensor_copy(cpT, bank(5, 2, T)).then_inc(S("c_pt"), 1)
                if i is not None:
                    evac(1, kq[:, 2:4])
                    split(1)
                    ev.take(2)
                if j is not None:
                    low(2 * j + YX, bank(6, 2, T), "c_hi", j + 1, "c_lo")

            phase(cross, 4, (0, 1, 2), 2)

            sq_, sk_ = cells(0, 2, T), cells(512, 2, T)
            sp_, sn, sls = cells(2304, 2, 384), cells(3072, 2, 384), cells(3840, 2, 384)

            def diagonals(v, heads):
                if heads == 1:
                    return v.rearrange("p (b c) -> p b c", b=3)[:, 0:3:2]
                return v.rearrange("p h (b c) -> p h b c", b=3)[:, :, 0:3:2]

            def stick(i, j):
                if i is not None:
                    split(2)
                if j is not None:
                    z = ps[:, 3:5, 0:384]
                    dve.wait_ge(S("s_abs"), j + 1)
                    chain(ts(sn, z, P ** -0.5, 0.0, ALU.mult, ALU.max))
                    dve.wait_ge(S("s_sp"), j + 1)
                    chain(tt(sn, sn, sp_, ALU.add))
                    chain(stt(sls, z, P ** -0.5, sn, ALU.mult, ALU.subtract))
                    tt(diagonals(sn, 2), diagonals(sn, 2), bc(diagonals(strict3, 1), 2), ALU.mult)\
                        .then_inc(S("s_nm"), 1)
                if i is not None:
                    evac(0, sq_)
                    split(0)
                if j is not None:
                    dve.wait_ge(S("s_lt"), j + 1)
                    tt(sls, sls, ps[:, 5:7, 0:384], ALU.subtract).then_inc(S("s_la"), 1)
                    dve.wait_ge(S("s_A"), j + 1)
                    tt(diagonals(sp_, 2), diagonals(sp_, 2), bc(diagonals(strict3, 1), 2), ALU.mult)\
                        .then_inc(S("s_Am"), 1)
                if i is not None:
                    evac(1, sk_)
                    split(1)
                    ev.take(2)
                if j is not None:
                    low(2 * j + YSB, bank(7, 2, T), "s_hi", j + 1, "s_lo")

            phase(stick, 4, (0, 1, 2), 3)

            qkp, cv, sg, mo = cells(0, 4, 260), cells(1040, 4, T), cells(2064, 4, T), cells(3600, 2, T)
            mbc, w_, sc, me, mhm, mr = (cells(4112, 2, T), cells(4624, 384), cells(5008, 384), cells(5392, T),
                                        cells(5648, 2, T), cells(6672, T))

            def conv(pad, dst, name, tiles, stride, cols):
                for n in cols:
                    last = ts(dst[:, n], pad[:, n, 0:T], pc("conv_w" + name, tiles[n]), pc("conv_b" + name, tiles[n]),
                              ALU.mult, ALU.add)
                for m in range(1, 4):
                    chain(last)
                    for n in cols:
                        last = stt(dst[:, n], pad[:, n, m:m + T], pc("conv_w" + name, tiles[n] + stride * m),
                                   dst[:, n], ALU.mult, ALU.add)
                return last

            chain(V.memset(qkp[:, :, 0:3], 0.0))

            def mlstm(i, j):
                if i is not None:
                    split(2)
                if j is not None:
                    dve.wait_ge(S("m_bc"), 16 * j + 16)
                    for s, (lo, hi, at) in enumerate(((0, T, 0), (P, T, T))):
                        ac = acol[:, s, j:j + 1] if isinstance(j, int) else acol[:, s, bass.ds(j, 1)]
                        last = ts(w_[:, at:at + hi - lo], mbc[:, 0, lo:hi], ac, 0.0, ALU.add, ALU.min)
                    last.then_inc(S("m_w0"), 1)
                    dve.wait_ge(S("m_w"), j + 1)
                    chain(tt(diagonals(w_, 1), diagonals(w_, 1), diagonals(incl3, 1), ALU.mult))
                    dve.wait_ge(S("m_s"), j + 1)
                    stt(sc, bank(3, 384), 1.0 / 16, w_, ALU.mult, ALU.mult).then_inc(S("m_sc"), 1)
                if i is not None:
                    ev.take(0)
                    evac(1, qkp[:, 2:4, 3:259])
                    split(1)
                    split(0)
                    need(dve, "m_s", i)
                    dve.wait_ge(S("bank0"), ev.banks(0))
                    dve.wait_ge(S("bank1"), ev.banks(1))
                    conv(qkp, cv, "", [2 * i, 2 * i + 1, 2 * i + 8, 2 * i + 9], 16, range(4))\
                        .then_inc(S("m_cv"), 1)
                if j is not None:
                    dve.wait_ge(S("m_abs"), j + 1)
                    dve.wait_ge(S("m_e"), j + 1)
                    chain(tt(mr, mr, me, ALU.max))
                    chain(V.reciprocal(mr, mr))
                    dve.wait_ge(S("m_num"), j + 1)
                    tt(mhm, bank(5, 2, T), bc(mr, 2), ALU.mult).then_inc(S("m_hm"), 1)
                if i is not None:
                    dve.wait_ge(S("m_sg"), i + 1)
                    tt(cv, cv, sg, ALU.mult).then_inc(S("m_qk"), 1)
                    split(1)
                    ev.take(2)
                    ev.take(1)
                if j is not None:
                    dve.wait_ge(S("m_r"), j + 1)
                    for c in range(2):
                        last = stt(mhm[:, c], mhm[:, c], pc("ml_norm_g", 2 * j + c), mr, ALU.mult, ALU.mult)
                    chain(last)
                    dve.wait_ge(S("m_o"), j + 1)
                    tt(mhm, mhm, mo, ALU.mult).then_inc(S("m_y"), 1)
                    low(2 * j + YML, mhm, "m_hi", j + 1, "m_lo")

            phase(mlstm, 4, (0, 1, 2, 1), 1 + 2 + 1 + 3)

            gt = cells(0, 2, T)

            def gated(first, last_=None, proj=(1,)):
                def body(i):
                    if len(proj) == 1:
                        split(0)
                    dve.wait_ge(S("bank0"), ev.banks(0) + 1)
                    ev.take(0)
                    if len(proj) == 1:
                        dve.wait_ge(S("unit1"), ev.take(1) + 1)
                        tt(gt, gt, bank(1, 2, CW), ALU.mult).then_inc(S("bank1"), 1)
                        dve.wait_ge(S("bank1"), ev.banks(1))
                    else:
                        for s in (2, 0, 1):
                            split(s)
                        ev.take(1, False)
                        dve.wait_ge(S("unit2"), ev.take(2, False) + 1)
                        tt(gt, gt, ps[:, 3:5, 0:T], ALU.mult).then_inc(S("q_proj"), 1)
                        dve.wait_ge(S("q_proj"), i + 2)
                    dst = rows(mix, 2 * i, 2)
                    if first:
                        V.tensor_copy(dst, gt).then_inc(S("p_used"), 1)
                    else:
                        tt(dst, dst, gt, ALU.add).then_inc(S("p_used"), 1)
                    if len(proj) == 1:
                        split(1)
                    if last_ is not None:
                        low(2 * i + M0, dst, "mix_hi", i + last_ + 1, "mix_lo")
                return body

            for n in range(3):
                loop(gated(n == 0, 0 if n == 2 else None), 4, (0, 1))

            def four(dst, add):
                for b, s in enumerate((0, 1, 2, 1)):
                    split((2, 1, 0, 1)[b])
                    dve.wait_ge(S(f"unit{s}"), ev.take(s) + 1)
                    d = dst[:, 2 * b:2 * b + 2]
                    last = tt(d, d, bank(s, 2, CW), ALU.add) if add else V.tensor_copy(d, bank(s, 2, CW))
                    last.then_inc(S(f"bank{s}"), 1)

            def norm(n, src, g, at=None, splits=0):
                t, r = cells(2048, KT, T), cells(4096, T)
                dve.wait_ge(S("n_r"), n + 1)
                for k in range(4):
                    v = slice(2 * k, 2 * k + 2)
                    tt(t[:, v], src[:, v], bc(r, 2), ALU.mult).then_inc(S("n_t"), 1)
                if at is None:
                    dve.wait_ge(S("n_t"), 4 * n + 4)
                    for k in range(KT):
                        last = stt(res[:, k], t[:, k], pc(g, k), res[:, k], ALU.mult, ALU.add)
                    return last
                for k in range(KT):
                    dve.wait_ge(S("n_hi"), KT * splits + k + 1)
                    stt(x_lo[:, at + k], t[:, k], pc(g, k), x_hi[:, at + k].bitcast(FP32),
                        ALU.mult, ALU.subtract).then_inc(S("n_lo"), 1)

            four(res, True)
            norm(0, res, "g_mlp", H0)

            def hidden(c0):
                def body(i):
                    for b, s in enumerate((0, 1, 2, 1)):
                        c = 4 * i + b
                        f, q = cells(512 * (b % 2), 2, T), cells(1024 + 512 * (b % 2), 2, T)
                        ev.take(s)
                        dve.wait_ge(S(f"bank{s}"), ev.banks(s))
                        tt(q, f, f, ALU.mult).then_inc(S("f_sq"), 1)
                        split((2, 1, 0, 1)[b])
                        low(2 * c + U0, q, "f_hi", c + c0 + 1, "f_lo")
                return body

            loop(hidden(0), 4, (0, 1, 2, 1))

            def deep(dst, add, kb, last_=False):
                def body(i):
                    for b in range(2 * kb):
                        s = (0, 1, 2, 1)[b % 4]
                        if not (last_ and b >= 2 * kb - 2):
                            split((2, 1, 0, 1)[b % 4])
                        n = ev.take(s, False)
                        if b % kb == kb - 1:
                            c = b // kb
                            dve.wait_ge(S(f"unit{s}"), n + 1)
                            d, v = rows(dst, 4 * i + 2 * c, 2), ps[:, 3 + 2 * c:5 + 2 * c, 0:T]
                            last = tt(d, d, v, ALU.add) if add else V.tensor_copy(d, v)
                            last.then_inc(S(f"deep{c}"), 1)
                return body

            loop(deep(res, True, 4), 2, (0, 1, 2, 1) * 2, 0, ())

            dve.wait_ge(S("deep1"), 3)
            norm(1, res, "norm_mix_pre_w_2", H0, 1)
            dve.wait_ge(S("dt_z"), 1)
            tt(dtz, bank(4, 2, 32), bc(dtb, 2), ALU.add).then_inc(S("dt_b"), 1)
            dve.wait_ge(S("dt_sp"), 1)
            chain(stt(dtc, dtz, 0.0, la, ALU.max, ALU.add))
            dve.wait_ge(S("dt_a"), 1)
            chain(ts(neg_a, neg_a, -1.0, None, ALU.mult))
            tt(la, dtc, bc(neg_a, 2), ALU.mult).then_inc(S("dt_la"), 1)
            one, acs = cells(6400, T)[0:32], cells(5120, T)[0:32]
            chain(V.memset(one, 1.0))
            dve.wait_ge(S("dt_t"), 1)
            V.tensor_tensor_scan(acs, one, bank(5, T)[0:32], 0.0, ALU.mult, ALU.add).then_inc(S("dt_rows"), 1)
            dve.wait_ge(S("dt_ct"), 1)
            ts(nacs, bank(6, 2, 32), -1.0, None, ALU.mult).then_inc(S("dt_col"), 1)

            aq, ak, abias, ap_ = cells(0, 2, T), cells(512, 2, T), cells(1536, 4, 384), cells(3072, 4, 384)

            def att(i, j):
                if i is not None:
                    split(2)
                if j is not None:
                    dve.wait_ge(S("a_bias"), 16 * j + 16)
                    dve.wait_ge(S("a_l"), j + 1)
                    stt(ap_, ps[:, 3:7, 0:384], 0.125, abias, ALU.mult, ALU.add).then_inc(S("a_b"), 1)
                    dve.wait_ge(S("a_b"), j + 1)
                    V.tensor_reduce(ax[:, 0:4], ap_[:, :, 0:P], AXX, ALU.max, negate=True)
                    V.tensor_reduce(ax[:, 4:8], ap_[:, :, P:384], AXX, ALU.max, negate=True)\
                        .then_inc(S("a_mx"), 1)
                if i is not None:
                    evac(0, aq)
                    split(0)
                if j is not None:
                    dve.wait_ge(S("a_p"), j + 1)
                    chain(V.reciprocal(ax[:, 16:24], ax[:, 8:16]))
                    for t, v in enumerate((slice(0, P), slice(P, 384))):
                        r = bc(ax[:, 16 + 4 * t:20 + 4 * t], v.stop - v.start, 2)
                        last = tt(ap_[:, :, v], ap_[:, :, v], r, ALU.mult)
                    last.then_inc(S("a_pn"), 1)
                if i is not None:
                    evac(1, ak)
                    split(1)
                    ev.take(2)
                if j is not None:
                    low(2 * j + YAT, bank(7, 2, T), "a_hi", j + 1, "a_lo")

            phase(att, 3, (0, 1, 2), 1)

            dxp, dcv, dsg, dz = cells(0, 4, 260), cells(1040, 4, T), cells(2064, 4, T), cells(3088, 2, T)
            dab, dcb, dxd, dec, dr, dy = (cells(3600, 4, T), cells(4624, 384), cells(5008, 2, T),
                                          cells(5520, 4, 384), cells(4624, T), cells(7056, 2, T))

            def columns(v, at, n):
                return v[:, at:at + n] if isinstance(at, int) else v[:, bass.ds(at, n)]

            chain(V.memset(dxp[:, :, 0:3], 0.0))

            def ssm(i, j):
                if i is not None:
                    split(2)
                if j is not None:
                    dve.wait_ge(S("d_bc"), 16 * j + 16)
                    for h in range(4):
                        for s, (lo, hi, at) in enumerate(((0, T, 0), (P, T, T))):
                            last = ts(dec[:, h, at:at + hi - lo], dab[:, h, lo:hi],
                                      columns(nacs[:, s], 4 * j + h, 1), 0.0, ALU.add, ALU.min)
                    last.then_inc(S("d_d"), 1)
                    dve.wait_ge(S("d_cb"), j + 1)
                    tt(dcb, bank(3, 384), incl3, ALU.mult)
                    for t in range(2):
                        last = tt(dxd[:, t].rearrange("p (h c) -> p h c", h=4),
                                  bank(4, 2, T)[:, t].rearrange("p (h c) -> p h c", h=4),
                                  bc(columns(dtc[:, t], 4 * j, 4), 64, 2), ALU.mult)
                    chain(last)
                    for c in range(2):
                        ts(dy[:, c], dcv[:, c], columns(skip, 2 * j + c, 1), None, ALU.mult)
                    dve.wait_ge(S("d_e"), j + 1)
                    tt(dec, dec, bc(dcb, 4), ALU.mult).then_inc(S("d_L"), 1)
                if i is not None:
                    split(0)
                    ev.take(0)
                    evac(1, dxp[:, 2:4, 3:259])
                    dve.wait_ge(S("bank0"), ev.banks(0))
                    dve.wait_ge(S("bank1"), ev.banks(1))
                    conv(dxp, dcv, "_2", [2 * i, 2 * i + 1, i + 16, i + 24], 32, range(4)).then_inc(S("d_cv"), 1)
                    split(1)
                if j is not None:
                    dve.wait_ge(S("d_yp"), j + 1)
                    chain(tt(dy, dy, bank(5, 2, T), ALU.add))
                    tt(dy, dy, dz, ALU.mult).then_inc(S("d_y"), 1)
                if i is not None:
                    dve.wait_ge(S("d_sg"), i + 1)
                    tt(dcv, dcv, dsg, ALU.mult).then_inc(S("d_xc"), 1)
                    dve.wait_ge(S("d_zs"), i + 1)
                    tt(dz, dz, bank(2, 2, CW), ALU.mult).then_inc(S("bank2"), 1)
                    ev.take(2)
                if j is not None:
                    dve.wait_ge(S("d_r"), j + 1)
                    for c in range(2):
                        last = stt(dy[:, c], dy[:, c], pc("ssm_norm_w_2", 2 * j + c), dr, ALU.mult, ALU.mult)
                    last.then_inc(S("d_yn"), 1)
                    low(2 * j + YSS, dy, "d_hi", j + 1, "d_lo")

            phase(ssm, 8, (0, 1, 2), 1 + 1 + 3)
            loop(gated(True), 4, (0, 1))
            loop(gated(False, 4, (1, 2)), 4, (0, 1, 2), 0, (0,))
            four(mix, False)
            norm(2, mix, "norm_mix_post_w_2").then_inc(S("r_post"), 1)
            dve.wait_ge(S("r_post"), 1)
            norm(3, res, "norm_ffn_pre_w_2", H0, 2)
            loop(hidden(16), 4, (0, 1, 2, 1))
            deep(mix, False, 4)(0)
            deep(mix, False, 4, True)(1)
            norm(4, mix, "norm_ffn_post_w_2").then_inc(S("end"), 1)
            for t in range(2):
                for b in range(2):
                    dve.wait_ge(S("end_t"), 2 * t + b + 1)
                    last = V.tensor_copy(cells(0, 2, D)[:, t, 512 * b:512 * b + 512], bank(3 + 2 * t + b, 512))
            last.then_inc(S("y_ready"), 1)

        @block.tensor
        def _(pe):
            sl = Slots()
            FP, TOK = False, True

            def mm(o, l, r, start=True, stop=True):
                return nc.tensor.matmul(o, l, r, start=start, stop=stop)

            def tr(o, i):
                return nc.tensor.transpose(o, i, ident[0:i.shape[0], 0:i.shape[0]])

            def unit_half(s, o, at, tok, nk=KT):
                last = products(pe, s, o, at, tok, nk)
                if o == 1:
                    last.then_inc(S(f"unit{s}"), 1)

            def unit(s, at, tok=FP, nk=KT):
                begin(pe, sl, s)
                unit_half(s, 0, at, tok, nk)
                unit_half(s, 1, at, tok, nk)

            pe.wait_ge(S("cst_in"), 16)
            pe.wait_ge(S("prow_in"), 16 * sum(len(t) for t in PARAM_TILES))
            prow = cells(4096, 3, P)
            for t in range(3):
                last = tr(bank(7, 3, P)[:, t], prow[:, t])
            last.then_inc(S("pcol_t"), 1)
            xn = cells(4480, 2, D)
            mtok, xtok = cells(2048, 2, D), cells(0, 2, D)

            def turned(src, b, name):
                for kt in (2 * b, 2 * b + 1):
                    for t in range(2):
                        last = tr(bank(b, 2, T)[:, kt % 2, t * P:(t + 1) * P], src[:, t, kt * P:(kt + 1) * P])
                last.then_inc(S(name), 1)

            pe.wait_ge(S("xn"), 1)
            for b in range(4):
                turned(xn, b, "h_t")
            pe.wait_ge(S("mn"), 1)
            for b in range(4):
                pe.wait_ge(S("h_lo"), b + 1)
                turned(mtok, b, "h_t")
            for b in range(4):
                pe.wait_ge(S("h_lo"), b + 5)
                turned(xtok, b, "res_t")
            pe.wait_ge(S("gate_in"), 32)
            for t in range(2):
                for k in range(KT):
                    for m, xt in enumerate((x_hi, x_lo)):
                        last = mm(bank(4, 2, 8)[:, t], xt[:, H0 + k, t * P:(t + 1) * P].bitcast(FP32), wif[:, k],
                                  k == 0 and m == 0, k == KT - 1 and m == 1)
            last.then_inc(S("g_z"), 1)
            pe.wait_ge(S("g_lf"), 1)
            for part in range(2):
                for t in range(2):
                    last = tr(bank(5, 2, T)[0:4, part, t * P:(t + 1) * P], gt1[:, t, 4 * part:4 * part + 4])
            last.then_inc(S("g_t"), 1)
            pe.wait_ge(S("g_rows"), 1)
            arow = cells(5632, T)
            for t in range(2):
                last = tr(bank(6, 2, 4)[:, t], arow[0:4, t * P:(t + 1) * P])
            last.then_inc(S("g_ct"), 1)
            pe.wait_ge(S("res"), 4)
            pe.wait_ge(S("g_col"), 1)

            kq, v, sq, kqn, p, pT = (cells(0, 4, T), cells(1024, 2, T), cells(1536, 4, T), cells(3072, 4, T),
                                     cells(4096, 2, T), cells(4608, 2, T))

            def cross(i, j):
                evacuated = [sl.banks(s) for s in range(SLOTS)]
                if i is not None:
                    begin(pe, sl, 0)
                    unit_half(0, 0, M0, FP)
                if j is not None:
                    pe.wait_ge(S("c_sq"), j + 1)
                    for n in range(4):
                        last = mm(bank(3, 2, T)[:, n // 2], ones, sq[:, n], n % 2 == 0, n % 2 == 1)
                    last.then_inc(S("c_ss"), 1)
                if i is not None:
                    unit_half(0, 1, M0, FP)
                    begin(pe, sl, 1)
                    unit_half(1, 0, H0, FP)
                if j is not None:
                    pe.wait_ge(S("c_n"), j + 1)
                    for t in range(2):
                        for d in range(2):
                            last = mm(bank(4, 2, T)[:, t], kqn[:, 2 + d, t * P:(t + 1) * P], kqn[:, d],
                                      d == 0, d == 1)
                    last.then_inc(S("c_lg"), 1)
                if i is not None:
                    unit_half(1, 1, H0, FP)
                    begin(pe, sl, 2)
                    unit_half(2, 0, M0, TOK)
                if j is not None:
                    pe.wait_ge(S("c_pn"), j + 1)
                    for m in range(2):
                        for t in range(2):
                            last = tr(bank(5, 2, T)[:, m, t * P:(t + 1) * P], p[:, t, m * P:(m + 1) * P])
                    last.then_inc(S("c_t"), 1)
                if i is not None:
                    unit_half(2, 1, M0, TOK)
                if j is not None:
                    pe.wait_ge(S("c_pt"), j + 1)
                    need(pe, "bank2", evacuated[2])
                    for d in range(2):
                        for m in range(2):
                            last = mm(bank(6, 2, T)[:, d], v[:, m, d * P:(d + 1) * P], pT[:, m], m == 0, m == 1)
                    last.then_inc(S("c_y"), 1)

            def phase(body, trips, pattern):
                body(0, None)
                sl.enter(pattern, 0)
                with pe.Fori(0, trips - 1) as j:
                    sl.trip = j
                    body(j + 1, j)
                sl.leave(trips - 1)
                body(None, trips - 1)

            phase(cross, 4, (0, 1, 2))

            sq_, sk_, sv_ = cells(0, 2, T), cells(512, 2, T), cells(1024, 2, T)
            sn, sA = cells(3072, 2, 384), cells(2304, 2, 384)

            def stick(i, j):
                evacuated = [sl.banks(s) for s in range(SLOTS)]
                if i is not None:
                    begin(pe, sl, 0)
                    unit_half(0, 0, H0, FP)
                if j is not None:
                    need(pe, "bank0", evacuated[0])
                    need(pe, "bank1", evacuated[1])
                    for h in range(2):
                        mm(bank(3 + h, 384)[:, 0:T], sk_[:, h, 0:P], sq_[:, h, :])
                        last = mm(bank(3 + h, 384)[:, T:384], sk_[:, h, P:T], sq_[:, h, P:T])
                    last.then_inc(S("s_z"), 1)
                if i is not None:
                    unit_half(0, 1, H0, FP)
                    begin(pe, sl, 1)
                    unit_half(1, 0, H0, FP)
                    unit_half(1, 1, H0, FP)
                if j is not None:
                    pe.wait_ge(S("s_nm"), j + 1)
                    for h in range(2):
                        mm(bank(5 + h, 384)[:, 0:T], later, sn[:, h, 0:T], True, False)
                        mm(bank(5 + h, 384)[:, P:T], ones, sn[:, h, T:384], False, True)
                        last = mm(bank(5 + h, 384)[:, T:384], later, sn[:, h, T:384])
                    last.then_inc(S("s_lt"), 1)
                if i is not None:
                    begin(pe, sl, 2)
                    unit_half(2, 0, H0, TOK)
                    unit_half(2, 1, H0, TOK)
                if j is not None:
                    pe.wait_ge(S("s_Am"), j + 1)
                    need(pe, "bank2", evacuated[2])
                    for h in range(2):
                        mm(bank(7, 2, T)[:, h], sv_[:, 0, h * P:(h + 1) * P], sA[:, h, 0:T], True, False)
                        last = mm(bank(7, 2, T)[:, h, P:T], sv_[:, 1, h * P:(h + 1) * P], sA[:, h, T:384],
                                  False, True)
                    last.then_inc(S("s_y"), 1)

            phase(stick, 4, (0, 1, 2))

            cv, mv, w_, sc, msq = cells(1040, 4, T), cells(3088, 2, T), cells(4624, 384), cells(5008, 384), \
                cells(6160, 2, T)

            def mlstm(i, j):
                evacuated = [sl.banks(s) for s in range(SLOTS)]
                if i is not None:
                    begin(pe, sl, 0)
                    unit_half(0, 0, H0, FP)
                if j is not None:
                    pe.wait_ge(S("m_qk"), j + 1)
                    for d in range(2):
                        mm(bank(3, 384)[:, 0:T], cv[:, 2 + d, 0:P], cv[:, d, :], d == 0, d == 1)
                    for d in range(2):
                        last = mm(bank(3, 384)[:, T:384], cv[:, 2 + d, P:T], cv[:, d, P:T], d == 0, d == 1)
                    last.then_inc(S("m_s"), 1)
                if i is not None:
                    unit_half(0, 1, H0, FP)
                    begin(pe, sl, 1)
                    unit_half(1, 0, H0, FP)
                    unit_half(1, 1, H0, FP)
                    begin(pe, sl, 2)
                    unit_half(2, 0, H0, TOK)
                if j is not None:
                    pe.wait_ge(S("m_sc"), j + 1)
                    need(pe, "bank2", evacuated[2])
                    mm(bank(4, T), ones, sc[:, 0:T], True, False)
                    mm(bank(4, T)[:, P:T], ones, sc[:, T:384], False, True).then_inc(S("m_den"), 1)
                    for d in range(2):
                        mm(bank(5, 2, T)[:, d], mv[:, 0, d * P:(d + 1) * P], sc[:, 0:T], True, False)
                        last = mm(bank(5, 2, T)[:, d, P:T], mv[:, 1, d * P:(d + 1) * P], sc[:, T:384], False, True)
                    last.then_inc(S("m_num"), 1)
                if i is not None:
                    unit_half(2, 1, H0, TOK)
                    begin(pe, sl, 1)
                    unit_half(1, 0, H0, FP)
                    unit_half(1, 1, H0, FP)
                if j is not None:
                    pe.wait_ge(S("m_sq"), j + 1)
                    for d in range(2):
                        last = mm(bank(6, T), ones, msq[:, d], d == 0, d == 1)
                    last.then_inc(S("m_ss"), 1)

            phase(mlstm, 4, (0, 1, 2, 1))

            def loop(body, trips, pattern, filled=None):
                sl.enter(pattern, 0, filled)
                with pe.Fori(0, trips) as i:
                    sl.trip = i
                    body(i)
                sl.leave(trips)

            def gated(at):
                def body(i):
                    unit(0, H0)
                    unit(1, at)
                return body

            for n, at in enumerate((YX, YSB, YML)):
                pe.wait_ge(S(("c_lo", "s_lo", "m_lo")[n]), 4)
                loop(gated(at), 4, (0, 1))

            def four(at):
                def body(i):
                    for s in (0, 1, 2, 1):
                        unit(s, at)
                return body

            def norm(n):
                for k in range(KT):
                    pe.wait_ge(S("n_sq"), KT * n + k + 1)
                    last = mm(bank(3, T), ones, cells(0, KT, T)[:, k], k == 0, k == KT - 1)
                last.then_inc(S("n_ss"), 1)

            def deep(kb, at, done0):
                def body(i):
                    for b in range(2 * kb):
                        s, c = (0, 1, 2, 1)[b % 4], b // kb
                        pe.wait_ge(S(f"w_split{s}"), sl.take(s, False) + 1)
                        if b % kb == 0:
                            pe.wait_ge(S(f"deep{c}"), i + done0 + 1)
                        for o in range(2):
                            last = products(pe, s, o, at + KT * (b % kb), FP, out_=bank(3 + 2 * c + o, T),
                                            start=b % kb == 0, stop=b % kb == kb - 1)
                        last.then_inc(S(f"unit{s}"), 1)
                return body

            pe.wait_ge(S("mix_lo"), 4)
            four(M0)(0)
            norm(0)
            pe.wait_ge(S("n_lo"), KT)
            loop(four(H0), 4, (0, 1, 2, 1))
            pe.wait_ge(S("f_lo"), 16)
            loop(deep(4, U0, 0), 2, (0, 1, 2, 1) * 2, ())

            norm(1)
            pe.wait_ge(S("n_lo"), 2 * KT)
            pe.wait_ge(S("dt_in"), 80)
            for t in range(2):
                for k in range(KT):
                    for m, xt in enumerate((x_hi, x_lo)):
                        last = mm(bank(4, 2, 32)[:, t], xt[:, H0 + k, t * P:(t + 1) * P].bitcast(FP32), wdt[:, k],
                                  k == 0 and m == 0, k == KT - 1 and m == 1)
            last.then_inc(S("dt_z"), 1)
            pe.wait_ge(S("dt_la"), 1)
            for t in range(2):
                last = tr(bank(5, T)[0:32, t * P:(t + 1) * P], la[:, t])
            last.then_inc(S("dt_t"), 1)
            pe.wait_ge(S("dt_rows"), 1)
            for t in range(2):
                last = tr(bank(6, 2, 32)[:, t], cells(5120, T)[0:32, t * P:(t + 1) * P])
            last.then_inc(S("dt_ct"), 1)
            pe.wait_ge(S("dt_col"), 1)

            aq, ak, av, ap_, apT = (cells(0, 2, T), cells(512, 2, T), cells(1024, 2, T), cells(3072, 4, 384),
                                    cells(4608, 4, 384))

            def head(h):
                return slice(64 * (h % 2), 64 * (h % 2) + 64), h // 2

            def att(i, j):
                evacuated = [sl.banks(s) for s in range(SLOTS)]
                if i is not None:
                    begin(pe, sl, 0)
                    unit_half(0, 0, H0, FP)
                if j is not None:
                    need(pe, "bank0", evacuated[0])
                    need(pe, "bank1", evacuated[1])
                    for h in range(4):
                        o, c = head(h)
                        mm(bank(3 + h, 384)[:, 0:P], aq[o, c, 0:P], ak[o, c, 0:P])
                        last = mm(bank(3 + h, 384)[:, P:384], aq[o, c, P:T], ak[o, c, :])
                    last.then_inc(S("a_l"), 1)
                if i is not None:
                    unit_half(0, 1, H0, FP)
                    begin(pe, sl, 1)
                    unit_half(1, 0, H0, FP)
                    unit_half(1, 1, H0, FP)
                if j is not None:
                    pe.wait_ge(S("a_pn"), j + 1)
                    for h in range(4):
                        for b in range(3):
                            last = tr(bank(3 + h, 384)[:, b * P:(b + 1) * P], ap_[:, h, b * P:(b + 1) * P])
                    last.then_inc(S("a_t"), 1)
                if i is not None:
                    begin(pe, sl, 2)
                    unit_half(2, 0, H0, TOK)
                    unit_half(2, 1, H0, TOK)
                if j is not None:
                    pe.wait_ge(S("a_pt"), j + 1)
                    need(pe, "bank2", evacuated[2])
                    for h in range(4):
                        o, c = head(h)
                        mm(bank(7, 2, T)[o, c], av[:, 0, 64 * h:64 * h + 64], apT[:, h, 0:T], True, False)
                        last = mm(bank(7, 2, T)[o, c, P:T], av[:, 1, 64 * h:64 * h + 64], apT[:, h, T:384],
                                  False, True)
                    last.then_inc(S("a_y"), 1)

            phase(att, 3, (0, 1, 2))

            dcv, dxd, dec, dsq = cells(1040, 4, T), cells(5008, 2, T), cells(5520, 4, 384), cells(5520, 2, T)

            def ssm(i, j):
                if i is not None:
                    begin(pe, sl, 0)
                    unit_half(0, 0, H0, FP)
                if j is not None:
                    pe.wait_ge(S("d_xc"), j + 1)
                    mm(bank(3, 384)[:, 0:T], dcv[:, 2, 0:P], dcv[:, 3, :])
                    mm(bank(3, 384)[:, T:384], dcv[:, 2, P:T], dcv[:, 3, P:T])
                    for t in range(2):
                        for c in range(2):
                            last = tr(bank(4, 2, T)[:, t, c * P:(c + 1) * P], dcv[:, c, t * P:(t + 1) * P])
                    last.then_inc(S("d_cb"), 1)
                if i is not None:
                    unit_half(0, 1, H0, FP)
                    begin(pe, sl, 1)
                    unit_half(1, 0, H0, FP)
                    unit_half(1, 1, H0, FP)
                if j is not None:
                    pe.wait_ge(S("d_L"), j + 1)
                    for h in range(4):
                        o, c = head(h)
                        mm(bank(5, 2, T)[o, c], dxd[:, 0, 64 * h:64 * h + 64], dec[:, h, 0:T], True, False)
                        last = mm(bank(5, 2, T)[o, c, P:T], dxd[:, 1, 64 * h:64 * h + 64], dec[:, h, T:384],
                                  False, True)
                    last.then_inc(S("d_yp"), 1)
                if i is not None:
                    begin(pe, sl, 2)
                    unit_half(2, 0, H0, FP)
                    unit_half(2, 1, H0, FP)
                if j is not None:
                    pe.wait_ge(S("d_sq"), j + 1)
                    for c in range(2):
                        last = mm(bank(6, T), ones, dsq[:, c], c == 0, c == 1)
                    last.then_inc(S("d_ss"), 1)

            pe.wait_ge(S("a_lo"), 3)
            phase(ssm, 8, (0, 1, 2))

            def gated_att(i):
                unit(0, H0)
                unit(1, YAT, FP, 6)

            def gated_ssm(i):
                unit(0, H0)
                pe.wait_ge(S("q_proj"), i + 1)
                for kb in range(2):
                    pe.wait_ge(S(f"w_split{1 + kb}"), sl.take(1 + kb, False) + 1)
                    for o in range(2):
                        last = products(pe, 1 + kb, o, YSS + KT * kb, FP, out_=bank(3 + o, T),
                                        start=kb == 0, stop=kb == 1)
                    last.then_inc(S(f"unit{1 + kb}"), 1)

            loop(gated_att, 4, (0, 1))
            pe.wait_ge(S("d_lo"), 8)
            loop(gated_ssm, 4, (0, 1, 2), (0,))
            pe.wait_ge(S("mix_lo"), 8)
            four(M0)(0)
            norm(2)
            norm(3)
            pe.wait_ge(S("n_lo"), 3 * KT)
            loop(four(H0), 4, (0, 1, 2, 1))
            pe.wait_ge(S("f_lo"), 32)
            loop(deep(4, U0, 2), 2, (0, 1, 2, 1) * 2, ())
            norm(4)
            pe.wait_ge(S("end"), 1)
            for t in range(2):
                for b in range(2):
                    for k in range(4):
                        last = tr(bank(3 + 2 * t + b, 4, P)[:, k], res[:, 4 * b + k, t * P:(t + 1) * P])
                    last.then_inc(S("end_t"), 1)


INPUTS = ("x", "mem", "g_mix", "w_in", "b_if", "b_gate", "conv_w", "conv_b", "ml_norm_g", "g_mem", "w_mem_kv",
          "q_norm_g", "k_norm_g", "w_sb_proj", "w_ml_proj", "w_x_proj", "w_out", "g_mlp", "w_ff1", "w_ff2",
          "norm_mix_pre_w_2", "w_in_2", "b_gate_2", "conv_w_2", "conv_b_2", "dt_bias_2", "a_log_2", "d_skip_2",
          "ssm_norm_w_2", "w_att_proj_2", "w_ssm_proj_2", "w_out_2", "norm_mix_post_w_2", "norm_ffn_pre_w_2",
          "w_up_2", "w_down_2", "norm_ffn_post_w_2")


def constants():
    import numpy as np
    p, f = np.arange(P)[:, None], np.arange(P)[None, :]
    one = np.ones((P, P))
    table = np.concatenate([p == f, one, p > f, f > p, one, f > p, f >= p, one, f >= p], 1)
    first = [2.0 ** (-(i + 1)) for i in range(8)]
    slopes = np.array(first + [2.0 ** (-0.5 * (i + 1)) for i in range(0, 8, 2)], np.float32)
    dist = np.arange(T)[:, None] - np.arange(T)[None, :]
    held = (dist >= 0) * ((dist <= 128) * 1 + (dist % 4 == 0) + (dist % 16 == 0))
    count = np.where(held > 0, np.log(np.maximum(held, 1)), -1e30)
    bias = -slopes[:, None, None].astype(np.float64) * np.maximum(dist, 0) + count
    bias = np.concatenate([bias[:, :P, :P], bias[:, P:, :]], 2)
    return (np.ascontiguousarray(table, dtype=np.float32),
            np.ascontiguousarray(bias.transpose(1, 0, 2), dtype=np.float32))


def kernel(**inputs):
    import numpy as np
    import concourse.bacc as bacc
    from concourse.bass_utils import run_bass_kernel_spmd as run

    nc = bacc.Bacc("TRN2", target_bir_lowering=False, num_devices=1)
    arrays, a = {}, {}
    given = {name: np.ascontiguousarray(inputs[name]) for name in INPUTS}
    given["consts"], given["att_bias"] = constants()
    for name, v in given.items():
        arrays[f"in_{name}"] = v
        a[name] = nc.dram_tensor(f"in_{name}", v.shape, mybir.dt.from_np(v.dtype), kind="ExternalInput").ap()
    a["rows"] = nc.dram_tensor("rows", (3, 32, T), FP32, kind="Internal").ap()
    out = nc.dram_tensor("out_0_dram", (1, T, D), FP32, kind="ExternalOutput").ap()
    build(nc, a, out)
    r = run(nc, [arrays], core_ids=[0])
    return r.results[0]["out_0_dram"]
```

```python
import concourse.bass as bass
from concourse import mybir
from contextlib import ExitStack

FP32 = mybir.dt.float32
FP32R = mybir.dt.float32r
ALU = mybir.AluOpType
ACT = mybir.ActivationFunctionType
AXX = mybir.AxisListType.X

P = 128
T = 256
D = 1024
KT = D // P
CW = 256
EPS = 1e-6
SLOTS = 3

SBQ, SBK, SBV, MLQ, MLK, MLV, MLO, MLI = (n * D for n in range(8))
XQ = MLI + 8
GATE = XQ + D
AQ, AK, AV = 0, 768, 1536
SZ = 2304
SX = SZ + 2048
SB_ = SX + 2048
SC = SB_ + 1024
SDT = SC + 1024
GATE2 = SDT + 32

H0, M0, Y0 = 0, 8, 16
YSB, YML, YX = Y0, Y0 + 8, Y0 + 16
YAT, YSS = Y0, Y0 + 6
U0 = 8
SQ = 4400
OPND = 40

PARAM_TILES = (
    (("conv_w_2", 128),),
    (("conv_w", 64), ("conv_b", 16), ("g_mix", 8), ("g_mem", 8), ("g_mlp", 8), ("ml_norm_g", 8),
     ("q_norm_g", 2), ("k_norm_g", 2), ("norm_mix_pre_w_2", 8)),
    (("b_gate", 24), ("conv_b_2", 32), ("ssm_norm_w_2", 16), ("b_gate_2", 16), ("norm_mix_post_w_2", 8),
     ("norm_ffn_pre_w_2", 8), ("norm_ffn_post_w_2", 8)),
)


def param_columns():
    col = {}
    for t, tile in enumerate(PARAM_TILES):
        at = 0
        for name, rows in tile:
            col[name] = t * P + at
            at += rows
    return col


class Slots:

    def __init__(self):
        self.units, self.fills = [0] * SLOTS, [0] * SLOTS
        self.unit_step, self.fill_step = [0] * SLOTS, [0] * SLOTS
        self.trip = 0

    def enter(self, pattern, trip, filled=None):
        filled = pattern if filled is None else filled
        self.unit_step = [pattern.count(s) for s in range(SLOTS)]
        self.fill_step = [filled.count(s) for s in range(SLOTS)]
        self.trip = trip

    def leave(self, trips):
        for s in range(SLOTS):
            self.units[s] += self.unit_step[s] * (trips - 1)
            self.fills[s] += self.fill_step[s] * (trips - 1)
        self.unit_step, self.fill_step = [0] * SLOTS, [0] * SLOTS

    def take(self, s, fills=True):
        n = self.units[s] + (self.trip * self.unit_step[s] if self.unit_step[s] else 0)
        self.units[s] += 1
        self.fills[s] += fills
        return n

    def banks(self, s):
        return self.fills[s] + (self.trip * self.fill_step[s] if self.fill_step[s] else 0)


class Chain:

    def __init__(self, eng, sem):
        self.eng, self.sem, self.n, self.per, self.trip = eng, sem, 0, 0, 0

    def __call__(self, instruction):
        instruction.then_inc(self.sem, 1)
        self.n += 1
        self.eng.wait_ge(self.sem, self.n + (self.trip * self.per if self.per else 0))

    def enter(self, trip, per):
        self.trip, self.per, self.start = trip, per, self.n

    def leave(self, trips):
        assert self.n - self.start == self.per, (self.n - self.start, self.per)
        self.n += self.per * (trips - 1)
        self.per = 0


def build(nc, a, out):
    ctx = ExitStack()
    with ctx:
        def sb(name, shape, dt=FP32):
            return ctx.enter_context(nc.sbuf_tensor(name, shape, dt))

        sems = {}

        def S(name):
            if name not in sems:
                sems[name] = ctx.enter_context(nc.semaphore(name))
            return sems[name]

        raw = sb("raw", [P, SLOTS, KT, CW])
        w_hi = sb("w_hi", [P, SLOTS, KT, CW], FP32R)
        w_lo = sb("w_lo", [P, SLOTS, KT, CW], FP32R)
        x_hi = sb("x_hi", [P, OPND, T], FP32R)
        x_lo = sb("x_lo", [P, OPND, T], FP32R)
        res = sb("res", [P, KT, T])
        mix = sb("mix", [P, KT, T])
        cst = sb("cst", [P, 3 * P + 2 * 384])
        ident, ones, later = (cst[:, n * P:(n + 1) * P] for n in range(3))
        strict3 = cst[:, 3 * P:3 * P + 384]
        incl3 = cst[:, 3 * P + 384:]
        pcol = sb("pcol", [P, 3 * P])
        small = sb("small", [P, 1024])
        arena = sb("arena", [P, 7600])
        ps = ctx.enter_context(nc.psum_tensor("ps", [P, 8, 512], FP32))
        col = param_columns()

        def cells(at, *dims):
            n = 1
            for d in dims:
                n *= d
            v = arena[:, at:at + n]
            if len(dims) == 2:
                return v.rearrange("p (a b) -> p a b", a=dims[0])
            if len(dims) == 3:
                return v.rearrange("p (a b c) -> p a b c", a=dims[0], b=dims[1])
            return v

        def bank(b, *dims):
            v = ps[:, b, :]
            if len(dims) == 2:
                return v[:, 0:dims[0] * dims[1]].rearrange("p (a b) -> p a b", a=dims[0])
            return v[:, 0:dims[0]]

        def pc(name, k=0):
            if isinstance(k, int):
                return pcol[:, col[name] + k:col[name] + k + 1]
            return pcol[:, bass.ds(k + col[name], 1)]

        def rows(t, at, n):
            return t[:, at:at + n, :] if isinstance(at, int) else t[:, bass.ds(at, n), :]

        def need(eng, name, n):
            if not isinstance(n, int) or n > 0:
                eng.wait_ge(S(name), n)

        eps = small[:, 0:1]
        bif = small[:, 8:16]
        wif = small[:, 16:80].rearrange("p (k c) -> p k c", k=KT)
        gz = small[:, 80:96].rearrange("p (t c) -> p t c", t=2)
        acol = small[:, 96:104].rearrange("p (t h) -> p t h", t=2)
        gt1 = small[:, 104:120].rearrange("p (t c) -> p t c", t=2)
        cx = small[:, 128:144]
        ssq = small[:, 144:160]
        wdt = small[:, 256:512].rearrange("p (k c) -> p k c", k=KT)
        dtb, neg_a = small[:, 512:544], small[:, 544:576]
        dtz, dtc, la, nacs = (small[:, n:n + 64].rearrange("p (t h) -> p t h", t=2) for n in (576, 640, 704, 768))
        skip = small[:, 832:848]
        ax = small[:, 848:880]

        w_in, w_in2 = a["w_in"][0], a["w_in_2"][0]

        def cols_of(w, k0, nk, at, n=CW):
            c = slice(at, at + n) if isinstance(at, int) else bass.ds(at, n)
            return w[k0 * P:(k0 + nk) * P, c].rearrange("(k p) n -> p k n", p=P)

        def load(eng, sl, s, parts):
            n = sl.take(s)
            need(eng, f"w_split{s}", n)
            for src, k0, nk, c0, nc_ in parts:
                eng.dma_start(raw[:, s, k0:k0 + nk, c0:c0 + nc_], src).then_inc(S(f"w_in{s}"), 16)

        def halves(w, k0, at, nk=KT):
            h = nk // 2
            return [(cols_of(w, k0 + n, h, at), n, h, 0, CW) for n in (h, 0)]

        def split_hi(act, sl, s):
            n = sl.take(s)
            act.wait_ge(S(f"w_in{s}"), n * 32 + 32)
            need(act, f"unit{s}", n)
            nc.scalar.copy(w_hi[:, s], raw[:, s]).then_inc(S(f"w_hi{s}"), 1)

        def split_lo(dve, sl, s):
            n = sl.take(s)
            dve.wait_ge(S(f"w_hi{s}"), n + 1)
            nc.vector.tensor_tensor(w_lo[:, s], raw[:, s], w_hi[:, s].bitcast(FP32), ALU.subtract)\
                .then_inc(S(f"w_split{s}"), 1)

        def products(pe, s, o, at, tok, nk=KT, out_=None, start=True, stop=True, lo=None):
            dst = bank(s, 2, CW)[:, o] if out_ is None else out_
            for k in range(nk):
                if lo is not None:
                    name, before, per = lo
                    pe.wait_ge(S(name), before + k // per + 1)
                for m, (wt, xt) in enumerate(((w_hi, x_hi), (w_hi, x_lo), (w_lo, x_hi))):
                    if tok:
                        l, r = xt[:, at + k, o * P:(o + 1) * P], wt[:, s, k, :]
                    else:
                        l, r = wt[:, s, k, o * P:(o + 1) * P], xt[:, at + k, :]
                    last = nc.tensor.matmul(dst, l, r, start=start and k == 0 and m == 0,
                                            stop=stop and k == nk - 1 and m == 2)
            return last

        def begin(pe, sl, s):
            need(pe, f"bank{s}", sl.banks(s))
            pe.wait_ge(S(f"w_split{s}"), sl.take(s) + 1)

        block = ctx.enter_context(nc.Block())

        @block.sync
        def _(sp):
            sl = Slots()
            xtok, mtok = cells(0, 2, D), cells(2048, 2, D)
            sp.dma_start(xtok, a["x"][0].rearrange("(t p) d -> p t d", p=P)).then_inc(S("x_in"), 16)
            sp.dma_start(mtok, a["mem"][0].rearrange("(t p) d -> p t d", p=P)).then_inc(S("m_in"), 16)

            def at(v):
                return v if isinstance(v, int) else sp.snap(v)

            def cross(i):
                yield 0, halves(a["w_mem_kv"][0], 0, at(i * CW))
                yield 1, halves(w_in, 0, at(i * CW + XQ))
                yield 2, halves(a["w_mem_kv"][0], 0, at(i * CW + D))

            def stick(i):
                for s, c in enumerate((SBQ, SBK, SBV)):
                    yield s, halves(w_in, 0, at(i * CW + c))

            def mlstm(i):
                for s, c in zip((0, 1, 2, 1), (MLQ, MLK, MLV, MLO)):
                    yield s, halves(w_in, 0, at(i * CW + c))

            def gated(w, wp, gate):
                def units(i):
                    yield 0, halves(w, 0, at(i * CW + gate))
                    yield 1, halves(wp, 0, at(i * CW))
                return units

            def plain(w, n):
                def units(i):
                    for b in range(n):
                        yield (0, 1, 2, 1)[b] if n == 4 else b, halves(w, 0, at((i * n + b) * CW))
                return units

            def deep(w, kb):
                def units(i):
                    for b in range(2 * kb):
                        yield (0, 1, 2, 1)[b % 4], halves(w, b % kb * KT, at((i * 2 + b // kb) * CW))
                return units

            def run(units, trips, pattern):
                sl.enter(pattern, 0)
                with sp.Fori(0, trips) as i:
                    sl.trip = i
                    for s, parts in units(i):
                        load(sp, sl, s, parts)
                sl.leave(trips)

            for s, parts in cross(0):
                load(sp, sl, s, parts)
            run(lambda i: cross(i + 1), 3, (0, 1, 2))
            run(stick, 4, (0, 1, 2))
            run(mlstm, 4, (0, 1, 2, 1))
            for w, g in (("w_x_proj", 2), ("w_sb_proj", 0), ("w_ml_proj", 1)):
                run(gated(w_in, a[w][0], GATE + g * D), 4, (0, 1))
            for s, parts in plain(a["w_out"][0], 4)(0):
                load(sp, sl, s, parts)
            run(plain(a["w_ff1"][0], 4), 4, (0, 1, 2, 1))
            run(deep(a["w_ff2"][0], 4), 2, (0, 1, 2, 1) * 2)

            def att(i):
                for s, c in enumerate((AQ, AK, AV)):
                    yield s, halves(w_in2, 0, at(i * CW + c))

            def ssm(i):
                yield 0, halves(w_in2, 0, at(i * CW + SX))
                yield 1, [(cols_of(w_in2, 0, KT, at(i * P + c), P), 0, KT, n * P, P)
                          for n, c in enumerate((SB_, SC))]
                yield 2, halves(w_in2, 0, at(i * CW + SZ))

            def gated_att(i):
                yield 0, halves(w_in2, 0, at(i * CW + GATE2))
                yield 1, halves(a["w_att_proj_2"][0], 0, at(i * CW), 6)

            def gated_ssm(i):
                yield 0, halves(w_in2, 0, at(i * CW + GATE2 + D))
                yield 1, halves(a["w_ssm_proj_2"][0], 0, at(i * CW))
                yield 2, halves(a["w_ssm_proj_2"][0], KT, at(i * CW))

            run(att, 3, (0, 1, 2))
            run(ssm, 8, (0, 1, 2))
            run(gated_att, 4, (0, 1))
            run(gated_ssm, 4, (0, 1, 2))
            for s, parts in plain(a["w_out_2"][0], 4)(0):
                load(sp, sl, s, parts)
            run(plain(a["w_up_2"][0], 4), 4, (0, 1, 2, 1))
            run(deep(a["w_down_2"][0], 4), 2, (0, 1, 2, 1) * 2)
            sp.wait_ge(S("y_ready"), 4)
            sp.dma_start(out[0].rearrange("(t p) d -> p t d", p=P), cells(0, 2, D)).then_inc(S("y_out"), 16)
            sp.wait_ge(S("y_out"), 16)

        @block.gpsimd
        def _(pool):
            nc.gpsimd.memset(cells(4096, 3, P), 0.0).then_inc(S("prow0"), 1)
            nc.gpsimd.memset(eps, EPS).then_inc(S("prow0"), 1)
            pool.dma_start(bif, a["b_if"].partition_broadcast(P)).then_inc(S("gate_in"), 16)
            pool.dma_start(wif, w_in[:, MLI:MLI + 8].rearrange("(k p) n -> p k n", p=P))\
                .then_inc(S("gate_in"), 16)

            pool.dma_start(wdt, w_in2[:, SDT:SDT + 32].rearrange("(k p) n -> p k n", p=P)).then_inc(S("dt_in"), 16)
            pool.dma_start(dtb, a["dt_bias_2"].partition_broadcast(P)).then_inc(S("dt_in"), 16)
            pool.dma_start(neg_a, a["a_log_2"].partition_broadcast(P)).then_inc(S("dt_in"), 16)
            for o in range(2):
                with nc.allow_non_contiguous_dma(reason="thirty-two scalars"):
                    pool.dma_start(skip[64 * o:64 * o + 64, :],
                                   a["d_skip_2"].rearrange("l (k o) -> l o k", o=2)[:, o, :].partition_broadcast(64))\
                        .then_inc(S("dt_in"), 16)

            pool.wait_ge(S("g_rows"), 1)
            pool.dma_start(a["rows"][0:2, 0:4].rearrange("r h t -> h r t"), cells(5120, 2, T)[0:4])\
                .then_inc(S("g_out"), 16)
            pool.wait_ge(S("g_out"), 16)

            def ml_rows(j):
                need(pool, "m_hm", j)
                pool.dma_start(cells(4112, 2, T), ml_src(j)).then_inc(S("m_bc"), 16)

            def ml_src(j):
                r = a["rows"][0:2, j:j + 1, :] if isinstance(j, int) else a["rows"][0:2, bass.ds(j, 1), :]
                return r.rearrange("r h t -> (r h) t").partition_broadcast(P)

            pool.wait_ge(S("s_lo"), 4)
            ml_rows(0)
            with pool.Fori(0, 3) as j:
                ml_rows(j + 1)

            def att_bias(j):
                need(pool, "a_b", j)
                h = slice(4 * j, 4 * j + 4) if isinstance(j, int) else bass.ds(4 * j, 4)
                pool.dma_start(cells(1536, 4, 384), a["att_bias"][:, h, :]).then_inc(S("a_bias"), 16)

            pool.wait_ge(S("dt_rows"), 1)
            pool.dma_start(a["rows"][2], cells(5120, T)[0:32]).then_inc(S("dt_out"), 16)
            pool.wait_ge(S("dt_out"), 16)
            pool.wait_ge(S("dt_col"), 1)
            att_bias(0)
            with pool.Fori(0, 2) as j:
                att_bias(j + 1)

            def decay_rows(j):
                need(pool, "d_d", j)
                h = slice(4 * j, 4 * j + 4) if isinstance(j, int) else bass.ds(4 * j, 4)
                pool.dma_start(cells(3600, 4, T), a["rows"][2, h, :].partition_broadcast(P)).then_inc(S("d_bc"), 16)

            pool.wait_ge(S("a_lo"), 3)
            decay_rows(0)
            with pool.Fori(0, 7) as j:
                decay_rows(j + 1)


        @block.scalar
        def _(act):
            sl, ev = Slots(), Slots()
            chain = Chain(act, S("act_chain"))
            A = nc.scalar.activation

            def inv_rms(dst, src, n):
                chain(A(dst, src, ACT.Ln, bias=eps, scale=1.0 / n))
                return A(dst, dst, ACT.Exp, scale=-0.5)

            def tables():
                act.preload_act_table_set("natural_log_exp_and_others")

            def evac(s, dst, func=ACT.Copy):
                act.wait_ge(S(f"unit{s}"), ev.take(s) + 1)
                A(dst, bank(s, 2, CW), func).then_inc(S(f"bank{s}"), 1)

            def split(s):
                split_hi(act, sl, s)

            def phase(body, trips, pattern, chained, first=True, last_=True):
                if first:
                    body(0, None)
                sl.enter(pattern, 0)
                ev.enter(pattern, 0)
                with act.Fori(0, trips - 1) as j:
                    sl.trip = ev.trip = j
                    chain.enter(j, chained)
                    body(j + 1, j)
                sl.leave(trips - 1)
                ev.leave(trips - 1)
                chain.leave(trips - 1)
                if last_:
                    body(None, trips - 1)

            def loop(body, trips, pattern, chained=0, filled=None):
                sl.enter(pattern, 0)
                ev.enter(pattern, 0, filled)
                with act.Fori(0, trips) as i:
                    sl.trip = ev.trip = i
                    chain.enter(i, chained)
                    body(i)
                sl.leave(trips)
                ev.leave(trips)
                chain.leave(trips)

            act.dma_start(cst[:, :], a["consts"]).then_inc(S("cst_in"), 16)
            prow = cells(4096, 3, P)
            act.wait_ge(S("prow0"), 2)
            for t, tile in enumerate(PARAM_TILES):
                at = 0
                for name, n in tile:
                    v = a[name][0]
                    v = v.rearrange("j (r c) -> (j r) c", c=P) if len(v.shape) == 2 else \
                        v.rearrange("(r c) -> r c", c=P)
                    act.dma_start(prow[at:at + n, t, :], v).then_inc(S("prow_in"), 16)
                    at += n
            tables()
            act.wait_ge(S("prow0"), 2)
            xtok, mtok = cells(0, 2, D), cells(2048, 2, D)
            junk = mix[:, :, :].rearrange("p (t c) n -> p t (c n)", t=2)
            for n, src in enumerate((xtok, mtok)):
                act.wait_ge(S(("x_in", "m_in")[n]), 16)
                for t in range(2):
                    last = A(junk[:, t], src[:, t], ACT.Square, accum_out=ssq[:, 2 * n + t:2 * n + t + 1])
                chain(last)
                inv_rms(ssq[:, 2 * n:2 * n + 2], ssq[:, 2 * n:2 * n + 2], D).then_inc(S("x_rs"), 1)
            split(0)
            act.wait_ge(S("pcol"), 1)
            for n, g in enumerate(("g_mix", "g_mem")):
                if n == 1:
                    split(1)
                for b in range(4):
                    act.wait_ge(S("h_t"), 4 * n + b + 1)
                    for k in range(2):
                        last = A(x_hi[:, (H0, M0)[n] + 2 * b + k], bank(b, 2, T)[:, k], ACT.Identity,
                                 scale=pc(g, 2 * b + k))
                    last.then_inc(S("h_hi"), 1)
            act.wait_ge(S("g_b"), 1)
            lf = gt1[:, :, 4:8]
            chain(A(lf, gz[:, :, 4:8], ACT.Abs))
            chain(A(lf, lf, ACT.Exp, scale=-1.0))
            A(lf, lf, ACT.Ln, bias=1.0).then_inc(S("g_sp"), 1)

            kq, cv_, csq, cr, cp = (cells(0, 4, T), cells(1024, 2, T), cells(1536, 4, T), cells(2560, 2, T),
                                    cells(4096, 2, T))

            def cross(i, j):
                kb, qb = ev.banks(0), ev.banks(1)
                if j is not None:
                    need(act, "bank0", kb)
                    need(act, "bank1", qb)
                    A(csq, kq, ACT.Square).then_inc(S("c_sq"), 1)
                if i is not None:
                    split(2)
                if j is not None:
                    act.wait_ge(S("c_ss"), j + 1)
                    inv_rms(cr, bank(3, 2, T), T).then_inc(S("c_r"), 1)
                if i is not None:
                    split(0)
                if j is not None:
                    act.wait_ge(S("c_mx"), j + 1)
                    for t in range(2):
                        last = A(cp[:, t], bank(4, 2, T)[:, t], ACT.Exp, bias=cx[:, t:t + 1], scale=1.0 / 16,
                                 accum_out=cx[:, 2 + t:3 + t])
                    last.then_inc(S("c_p"), 1)
                if i is not None:
                    split(1)
                if j is not None:
                    act.wait_ge(S("c_y"), j + 1)
                    A(rows(x_hi, 2 * j + YX, 2), bank(6, 2, T), ACT.Copy).then_inc(S("c_hi"), 1)
                if i is not None:
                    ev.take(0)
                    ev.take(1)
                    evac(2, cv_)

            act.wait_ge(S("res"), 4)
            phase(cross, 4, (0, 1, 2), 1, last_=False)
            cross(4, 3)

            sv_, se, sp_, sls = cells(1024, 2, T), cells(1536, 2, 384), cells(2304, 2, 384), cells(3840, 2, 384)

            def stick(i, j):
                if i is not None:
                    split(2)
                if j is not None:
                    act.wait_ge(S("s_z"), j + 1)
                    A(se, ps[:, 3:5, 0:384], ACT.Abs, scale=P ** -0.5).then_inc(S("s_abs"), 1)
                    act.wait_ge(S("s_abs"), j + 1)
                    chain(A(se, se, ACT.Exp, scale=-1.0))
                    A(sp_, se, ACT.Ln, bias=1.0).then_inc(S("s_sp"), 1)
                if i is not None:
                    split(0)
                if j is not None:
                    act.wait_ge(S("s_la"), j + 1)
                    A(sp_, sls, ACT.Exp).then_inc(S("s_A"), 1)
                if i is not None:
                    split(1)
                if j is not None:
                    act.wait_ge(S("s_y"), j + 1)
                    A(rows(x_hi, 2 * j + YSB, 2), bank(7, 2, T), ACT.Copy).then_inc(S("s_hi"), 1)
                if i is not None:
                    ev.take(0)
                    ev.take(1)
                    evac(2, sv_)

            phase(stick, 4, (0, 1, 2), 1, first=False)

            qkp, cv, sg, mv, mo = (cells(0, 4, 260), cells(1040, 4, T), cells(2064, 4, T), cells(3088, 2, T),
                                   cells(3600, 2, T))
            mbc, w_, me, mhm, msq, mr = (cells(4112, 2, T), cells(4624, 384), cells(5392, T), cells(5648, 2, T),
                                         cells(6160, 2, T), cells(6672, T))
            act.wait_ge(S("s_lo"), 4)

            def first_tap(pad, dst, name, tiles):
                act.wait_ge(S("bank0"), ev.banks(0))
                act.wait_ge(S("bank1"), ev.banks(1))
                for n in range(4):
                    last = A(dst[:, n], pad[:, n, 0:T], ACT.Identity, bias=pc("conv_b" + name, tiles[n]),
                             scale=pc("conv_w" + name, tiles[n]))
                return last

            act.wait_ge(S("m_pad"), 1)

            def mlstm(i, j):
                gates = ev.banks(1)
                if i is not None:
                    split(2)
                if j is not None:
                    act.wait_ge(S("m_w0"), j + 1)
                    A(w_, w_, ACT.Exp).then_inc(S("m_w"), 1)
                    A(me, mbc[:, 1], ACT.Exp).then_inc(S("m_e"), 1)
                if i is None:
                    fill(0)
                    fill(1)
                if i is not None:
                    evac(0, qkp[:, 0:2, 3:259])
                    split(1)
                    ev.take(1)
                    split(0)
                    need(act, "m_s", i)
                    first_tap(qkp, cv, "", [2 * i, 2 * i + 1, 2 * i + 8, 2 * i + 9]).then_inc(S("m_c0"), 1)
                if j is not None:
                    act.wait_ge(S("m_hm"), j + 1)
                    A(msq, mhm, ACT.Square).then_inc(S("m_sq"), 1)
                    if i is None:
                        fill(2)
                        tables()
                    act.wait_ge(S("m_ss"), j + 1)
                    inv_rms(mr, bank(6, T), T).then_inc(S("m_r"), 1)
                if i is not None:
                    evac(2, mv)
                    act.wait_ge(S("m_cv"), i + 1)
                    A(cv, cv, ACT.Silu).then_inc(S("m_qk"), 1)
                    split(1)
                if j is not None:
                    need(act, "bank1", gates)
                    A(mo, mo, ACT.Sigmoid).then_inc(S("m_o"), 1)
                    tables()
                    act.wait_ge(S("m_y"), j + 1)
                    A(rows(x_hi, 2 * j + YML, 2), mhm, ACT.Copy).then_inc(S("m_hi"), 1)
                    if i is None:
                        fill(3)
                else:
                    tables()
                if i is not None:
                    evac(1, mo)

            gt = cells(0, 2, T)

            def gated(bias, first, last_, proj=(1,), b_gate="b_gate"):
                def body(i):
                    if len(proj) == 1:
                        split(0)
                    act.wait_ge(S("unit0"), ev.take(0) + 1)
                    act.wait_ge(S("p_used"), i + first + 1)
                    for c in range(2):
                        last = A(gt[:, c], bank(0, 2, CW)[:, c], ACT.Sigmoid, bias=pc(b_gate, 2 * i + bias + c))
                    last.then_inc(S("bank0"), 1)
                    if len(proj) == 1:
                        split(1)
                        ev.take(1)
                    else:
                        for s in (2, 0, 1):
                            split(s)
                        for s in proj:
                            ev.take(s, False)
                    if last_:
                        act.wait_ge(S("p_used"), i + first + 2)
                        A(rows(x_hi, 2 * i + M0, 2), rows(mix, 2 * i, 2), ACT.Copy).then_inc(S("mix_hi"), 1)
                return body

            fill = gated(16, 0, False)
            phase(mlstm, 4, (0, 1, 2, 1), 1)
            for n, g in enumerate((0, 1)):
                loop(gated(8 * g, 4 + 4 * n, n == 1), 4, (0, 1))
            tables()

            def squares(src, at):
                A(rows(cells(SQ, KT, T), at, 2), rows(src, at, 2), ACT.Square).then_inc(S("n_sq"), 1)

            def high(src, g, b):
                for k in (2 * b, 2 * b + 1):
                    A(x_hi[:, H0 + k], src[:, k], ACT.Identity, scale=pc(g, k)).then_inc(S("n_hi"), 1)

            def inverse(n, power=-0.5):
                r = cells(4096, T)
                act.wait_ge(S("n_ss"), n + 1)
                chain(A(r, bank(7, T), ACT.Ln, bias=eps, scale=1.0 / D))
                A(r, r, ACT.Exp, scale=power).then_inc(S("n_r"), 1)

            def four_squared(dst, g=None):
                for b, s in enumerate((0, 1, 2, 1)):
                    split((2, 1, 0, 1)[b])
                    ev.take(s)
                    act.wait_ge(S(f"bank{s}"), ev.banks(s))
                    squares(dst, 2 * b)
                    if g is not None:
                        high(dst, g, b)

            four_squared(res, "g_mlp")
            inverse(0, -1.0)

            def hidden(c0):
                def body(i):
                    for b, s in enumerate((0, 1, 2, 1)):
                        act.wait_ge(S(f"unit{s}"), ev.take(s) + 1)
                        c = 4 * i + b
                        f = cells(512 * (b % 2), 2, T)
                        A(f, bank(s, 2, CW), ACT.Relu).then_inc(S(f"bank{s}"), 1)
                        split((2, 1, 0, 1)[b])
                        act.wait_ge(S("f_sq"), c + c0 + 1)
                        A(rows(x_hi, 2 * c + U0, 2), cells(1024 + 512 * (b % 2), 2, T), ACT.Copy)\
                            .then_inc(S("f_hi"), 1)
                return body

            loop(hidden(0), 4, (0, 1, 2, 1))

            def deep(dst, done0, last_=False):
                def body(i):
                    for b in range(8):
                        ev.take((0, 1, 2, 1)[b % 4], False)
                        if not (last_ and b >= 6):
                            split((2, 1, 0, 1)[b % 4])
                        if b % 4 == 3:
                            act.wait_ge(S(f"deep{b // 4}"), i + done0 + 2)
                            squares(dst, 4 * i + 2 * (b // 4))
                return body

            loop(deep(res, 0), 2, (0, 1, 2, 1) * 2, filled=())

            inverse(1)
            for b in range(4):
                act.wait_ge(S("n_t"), b + 1)
                high(cells(2048, KT, T), "norm_mix_pre_w_2", b)
            act.wait_ge(S("dt_in"), 80)
            A(neg_a, neg_a, ACT.Exp).then_inc(S("dt_a"), 1)

            def step_sizes():
                act.wait_ge(S("dt_b"), 1)
                chain(A(la, dtz, ACT.Abs))
                chain(A(la, la, ACT.Exp, scale=-1.0))
                A(la, la, ACT.Ln, bias=1.0).then_inc(S("dt_sp"), 1)

            av, ap_, apT = cells(1024, 2, T), cells(3072, 4, 384), cells(4608, 4, 384)

            def att(i, j):
                if i is not None:
                    split(2)
                    split(0)
                if j is not None:
                    act.wait_ge(S("a_mx"), j + 1)
                    for h in range(4):
                        for t, v in enumerate((slice(0, P), slice(P, 384))):
                            last = A(ap_[:, h, v], ap_[:, h, v], ACT.Exp, bias=ax[:, 4 * t + h:4 * t + h + 1],
                                     accum_out=ax[:, 8 + 4 * t + h:9 + 4 * t + h])
                    last.then_inc(S("a_p"), 1)
                if i is not None:
                    if j is None:
                        step_sizes()
                    split(1)
                if j is not None:
                    act.wait_ge(S("a_t"), j + 1)
                    A(apT, ps[:, 3:7, 0:384], ACT.Copy).then_inc(S("a_pt"), 1)
                    act.wait_ge(S("a_y"), j + 1)
                    A(rows(x_hi, 2 * j + YAT, 2), bank(7, 2, T), ACT.Copy).then_inc(S("a_hi"), 1)
                if i is not None:
                    ev.take(0)
                    ev.take(1)
                    evac(2, av)

            phase(att, 3, (0, 1, 2), 0)

            dxp, dcv, dsg, dz = cells(0, 4, 260), cells(1040, 4, T), cells(2064, 4, T), cells(3088, 2, T)
            dec, dsq, dr, dy = cells(5520, 4, 384), cells(5520, 2, T), cells(4624, T), cells(7056, 2, T)
            act.wait_ge(S("a_lo"), 3)
            act.wait_ge(S("m_pad"), 2)

            def ssm(i, j):
                if j is not None:
                    act.wait_ge(S("d_d"), j + 1)
                    A(dec, dec, ACT.Exp).then_inc(S("d_e"), 1)
                if i is None:
                    fill(0)
                    fill(1)
                if i is not None:
                    split(2)
                    evac(0, dxp[:, 0:2, 3:259])
                    split(0)
                    ev.take(1)
                    split(1)
                    need(act, "d_L", i)
                    first_tap(dxp, dcv, "_2", [2 * i, 2 * i + 1, i + 16, i + 24]).then_inc(S("d_c0"), 1)
                if j is not None:
                    act.wait_ge(S("d_y"), j + 1)
                    A(dsq, dy, ACT.Square).then_inc(S("d_sq"), 1)
                    if i is None:
                        fill(2)
                        tables()
                    act.wait_ge(S("d_ss"), j + 1)
                    inv_rms(dr, bank(6, T), T).then_inc(S("d_r"), 1)
                if i is not None:
                    act.wait_ge(S("d_cv"), i + 1)
                    A(dcv, dcv, ACT.Silu).then_inc(S("d_xc"), 1)
                    evac(2, dz, ACT.Silu)
                    tables()
                if j is not None:
                    act.wait_ge(S("d_yn"), j + 1)
                    A(rows(x_hi, 2 * j + YSS, 2), dy, ACT.Copy).then_inc(S("d_hi"), 1)
                    if i is None:
                        fill(3)

            fill = gated(0, 12, False, b_gate="b_gate_2")
            phase(ssm, 8, (0, 1, 2), 1)
            loop(gated(8, 16, True, (1, 2), "b_gate_2"), 4, (0, 1, 2), 0, (0,))
            tables()
            four_squared(mix)
            inverse(2)
            for b in range(4):
                act.wait_ge(S("r_post"), b + 1)
                squares(res, 2 * b)
                high(res, "norm_ffn_pre_w_2", b)
            inverse(3, -1.0)
            loop(hidden(16), 4, (0, 1, 2, 1))
            deep(mix, 2)(0)
            deep(mix, 2, True)(1)
            inverse(4)
            for b in range(2):
                act.wait_ge(S("end_t"), 2 * b + 2)
                A(cells(0, 2, D)[:, 1, 512 * b:512 * b + 512], bank(5 + b, 512), ACT.Copy).then_inc(S("y_ready"), 1)

        @block.vector
        def _(dve):
            sl, ev = Slots(), Slots()
            chain = Chain(dve, S("dve_chain"))
            V = nc.vector
            tt, ts, stt = V.tensor_tensor, V.tensor_scalar, V.scalar_tensor_tensor

            def split(s):
                split_lo(dve, sl, s)

            def evac(s, dst):
                dve.wait_ge(S(f"unit{s}"), ev.take(s) + 1)
                V.tensor_copy(dst, bank(s, 2, CW)).then_inc(S(f"bank{s}"), 1)

            def phase(body, trips, pattern, chained, first=True, last_=True):
                if first:
                    body(0, None)
                sl.enter(pattern, 0)
                ev.enter(pattern, 0)
                with dve.Fori(0, trips - 1) as j:
                    sl.trip = ev.trip = j
                    chain.enter(j, chained)
                    body(j + 1, j)
                sl.leave(trips - 1)
                ev.leave(trips - 1)
                chain.leave(trips - 1)
                if last_:
                    body(None, trips - 1)

            def loop(body, trips, pattern, chained=0, filled=None):
                sl.enter(pattern, 0)
                ev.enter(pattern, 0, filled)
                with dve.Fori(0, trips) as i:
                    sl.trip = ev.trip = i
                    chain.enter(i, chained)
                    body(i)
                sl.leave(trips)
                ev.leave(trips)
                chain.leave(trips)

            def bc(v, n, at=1):
                v = v.unsqueeze(at)
                return v.broadcast_to([*v.shape[:at], n, *v.shape[at + 1:]])

            def low(at, src, hi_name, n, lo_name, k=2):
                dve.wait_ge(S(hi_name), n)
                tt(rows(x_lo, at, k), src, rows(x_hi, at, k).bitcast(FP32), ALU.subtract).then_inc(S(lo_name), 1)

            for n, name in enumerate(("p_used", "q_proj", "deep0", "deep1")):
                V.memset(small[:, 900 + n:901 + n], 0.0).then_inc(S(name), 1)
            dve.wait_ge(S("pcol_t"), 1)
            V.tensor_copy(pcol[:, :], bank(7, 384)).then_inc(S("pcol"), 1)
            xtok, mtok, xn = cells(0, 2, D), cells(2048, 2, D), cells(4480, 2, D)
            dve.wait_ge(S("x_rs"), 1)
            for t in range(2):
                last = ts(xn[:, t], xtok[:, t], ssq[:, t:t + 1], None, ALU.mult)
            last.then_inc(S("xn"), 1)
            dve.wait_ge(S("x_rs"), 2)
            for t in range(2):
                last = ts(mtok[:, t], mtok[:, t], ssq[:, 2 + t:3 + t], None, ALU.mult)
            last.then_inc(S("mn"), 1)
            dve.wait_ge(S("pcol"), 1)
            for n, g in enumerate(("g_mix", "g_mem")):
                for b in range(4):
                    dve.wait_ge(S("h_hi"), 4 * n + b + 1)
                    for k in range(2):
                        at = (H0, M0)[n] + 2 * b + k
                        last = stt(x_lo[:, at], bank(b, 2, T)[:, k], pc(g, 2 * b + k), x_hi[:, at].bitcast(FP32),
                                   ALU.mult, ALU.subtract)
                    last.then_inc(S("h_lo"), 1)
            split(0)
            split(1)
            for b in range(4):
                dve.wait_ge(S("res_t"), b + 1)
                V.tensor_copy(res[:, 2 * b:2 * b + 2], bank(b, 2, T)).then_inc(S("res"), 1)
            dve.wait_ge(S("gate_in"), 32)
            dve.wait_ge(S("g_z"), 1)
            tt(gz, bank(4, 2, 8), bc(bif, 2), ALU.add).then_inc(S("g_b"), 1)
            dve.wait_ge(S("g_sp"), 1)
            stt(gt1[:, :, 4:8], gz[:, :, 4:8], 0.0, gt1[:, :, 4:8], ALU.min, ALU.subtract)
            V.tensor_copy(gt1[:, :, 0:4], gz[:, :, 0:4]).then_inc(S("g_lf"), 1)
            one, bsum, top, arow = (cells(n, T)[0:4] for n in (6400, 5888, 6144, 5632))
            outr = cells(5120, 2, T)[0:4]
            dve.wait_ge(S("g_t"), 1)
            chain(V.memset(one, 1.0))
            chain(V.tensor_tensor_scan(bsum, one, bank(5, 2, T)[0:4, 1], 0.0, ALU.mult, ALU.add))
            chain(tt(arow, bank(5, 2, T)[0:4, 0], bsum, ALU.subtract))
            chain(V.tensor_tensor_scan(top, arow, arow, 0.0, ALU.max, ALU.max))
            ts(outr[:, 0], top, -1.0, None, ALU.mult)
            stt(outr[:, 1], bsum, -1.0, top, ALU.mult, ALU.subtract).then_inc(S("g_rows"), 1)
            dve.wait_ge(S("g_ct"), 1)
            V.tensor_copy(acol, bank(6, 2, 4)).then_inc(S("g_col"), 1)

            kq, cr, kqn, cp, cpT = (cells(0, 4, T), cells(2560, 2, T), cells(3072, 4, T), cells(4096, 2, T),
                                    cells(4608, 2, T))

            def cross(i, j):
                if i is not None:
                    split(2)
                if j is not None:
                    dve.wait_ge(S("c_r"), j + 1)
                    for n in range(4):
                        g = pc(("k_norm_g", "q_norm_g")[n // 2], n % 2)
                        last = stt(kqn[:, n], kq[:, n], g, cr[:, n // 2], ALU.mult, ALU.mult)
                    last.then_inc(S("c_n"), 1)
                    dve.wait_ge(S("c_n"), j + 1)
                if i is not None:
                    evac(0, kq[:, 0:2])
                    split(0)
                if j is not None:
                    dve.wait_ge(S("c_lg"), j + 1)
                    chain(V.tensor_reduce(cx[:, 4:6], bank(4, 2, T), AXX, ALU.max, negate=True))
                    ts(cx[:, 0:2], cx[:, 4:6], 1.0 / 16, None, ALU.mult).then_inc(S("c_mx"), 1)
                    dve.wait_ge(S("c_p"), j + 1)
                    chain(V.reciprocal(cx[:, 6:8], cx[:, 2:4]))
                    for t in range(2):
                        last = ts(cp[:, t], cp[:, t], cx[:, 6 + t:7 + t], None, ALU.mult)
                    last.then_inc(S("c_pn"), 1)
                    dve.wait_ge(S("c_t"), j + 1)
                    V.tensor_copy(cpT, bank(5, 2, T)).then_inc(S("c_pt"), 1)
                if i is not None:
                    evac(1, kq[:, 2:4])
                    split(1)
                    ev.take(2)
                if j is not None:
                    low(2 * j + YX, bank(6, 2, T), "c_hi", j + 1, "c_lo")

            phase(cross, 4, (0, 1, 2), 2, last_=False)
            cross(4, 3)

            sq_, sk_ = cells(0, 2, T), cells(512, 2, T)
            sp_, sn, sls = cells(2304, 2, 384), cells(3072, 2, 384), cells(3840, 2, 384)

            def diagonals(v, heads):
                if heads == 1:
                    return v.rearrange("p (b c) -> p b c", b=3)[:, 0:3:2]
                return v.rearrange("p h (b c) -> p h b c", b=3)[:, :, 0:3:2]

            def stick(i, j):
                if i is not None:
                    split(2)
                if j is not None:
                    z = ps[:, 3:5, 0:384]
                    dve.wait_ge(S("s_abs"), j + 1)
                    chain(ts(sn, z, P ** -0.5, 0.0, ALU.mult, ALU.max))
                    dve.wait_ge(S("s_sp"), j + 1)
                    chain(tt(sn, sn, sp_, ALU.add))
                    chain(stt(sls, z, P ** -0.5, sn, ALU.mult, ALU.subtract))
                    tt(diagonals(sn, 2), diagonals(sn, 2), bc(diagonals(strict3, 1), 2), ALU.mult)\
                        .then_inc(S("s_nm"), 1)
                if i is not None:
                    evac(0, sq_)
                    split(0)
                if j is not None:
                    dve.wait_ge(S("s_lt"), j + 1)
                    tt(sls, sls, ps[:, 5:7, 0:384], ALU.subtract).then_inc(S("s_la"), 1)
                    dve.wait_ge(S("s_A"), j + 1)
                    tt(diagonals(sp_, 2), diagonals(sp_, 2), bc(diagonals(strict3, 1), 2), ALU.mult)\
                        .then_inc(S("s_Am"), 1)
                if i is not None:
                    evac(1, sk_)
                    split(1)
                    ev.take(2)
                if j is not None:
                    low(2 * j + YSB, bank(7, 2, T), "s_hi", j + 1, "s_lo")

            phase(stick, 4, (0, 1, 2), 3, first=False)

            qkp, cv, sg, mo = cells(0, 4, 260), cells(1040, 4, T), cells(2064, 4, T), cells(3600, 2, T)
            mbc, w_, sc, me, mhm, mr = (cells(4112, 2, T), cells(4624, 384), cells(5008, 384), cells(5392, T),
                                        cells(5648, 2, T), cells(6672, T))

            def conv(pad, dst, name, tiles, stride):
                for m in range(1, 4):
                    if m > 1:
                        chain(last)
                    for n in range(4):
                        last = stt(dst[:, n], pad[:, n, m:m + T], pc("conv_w" + name, tiles[n] + stride * m),
                                   dst[:, n], ALU.mult, ALU.add)
                return last

            V.memset(qkp[:, :, 0:3], 0.0).then_inc(S("m_pad"), 1)

            def mlstm(i, j):
                if i is not None:
                    split(2)
                if j is not None:
                    dve.wait_ge(S("m_bc"), 16 * j + 16)
                    for s, (lo, hi, at) in enumerate(((0, T, 0), (P, T, T))):
                        ac = acol[:, s, j:j + 1] if isinstance(j, int) else acol[:, s, bass.ds(j, 1)]
                        last = ts(w_[:, at:at + hi - lo], mbc[:, 0, lo:hi], ac, 0.0, ALU.add, ALU.min)
                    last.then_inc(S("m_w0"), 1)
                    dve.wait_ge(S("m_w"), j + 1)
                    chain(tt(diagonals(w_, 1), diagonals(w_, 1), diagonals(incl3, 1), ALU.mult))
                    if i is None:
                        fill(0)
                    dve.wait_ge(S("m_s"), j + 1)
                    stt(sc, bank(3, 384), 1.0 / 16, w_, ALU.mult, ALU.mult).then_inc(S("m_sc"), 1)
                if i is not None:
                    ev.take(0)
                    evac(1, qkp[:, 2:4, 3:259])
                    split(1)
                    split(0)
                else:
                    fill(1)
                if j is not None:
                    dve.wait_ge(S("m_den"), j + 1)
                    dve.wait_ge(S("m_e"), j + 1)
                    chain(stt(mr, bank(4, T), -1.0, me, ALU.mult, ALU.max))
                    chain(tt(mr, mr, bank(4, T), ALU.max))
                    chain(V.reciprocal(mr, mr))
                    dve.wait_ge(S("m_num"), j + 1)
                    tt(mhm, bank(5, 2, T), bc(mr, 2), ALU.mult).then_inc(S("m_hm"), 1)
                if i is None:
                    fill(2)
                if i is not None:
                    dve.wait_ge(S("m_c0"), i + 1)
                    conv(qkp, cv, "", [2 * i, 2 * i + 1, 2 * i + 8, 2 * i + 9], 16)\
                        .then_inc(S("m_cv"), 1)
                    ev.take(2)
                    ev.take(1)
                if j is not None:
                    dve.wait_ge(S("m_r"), j + 1)
                    for c in range(2):
                        last = stt(mhm[:, c], mhm[:, c], pc("ml_norm_g", 2 * j + c), mr, ALU.mult, ALU.mult)
                    chain(last)
                if i is not None:
                    split(1)
                if j is not None:
                    dve.wait_ge(S("m_o"), j + 1)
                    tt(mhm, mhm, mo, ALU.mult).then_inc(S("m_y"), 1)
                    low(2 * j + YML, mhm, "m_hi", j + 1, "m_lo")
                if i is None:
                    fill(3)

            gt = cells(0, 2, T)

            def gated(first, last_=None, proj=(1,)):
                def body(i):
                    if len(proj) == 1:
                        split(0)
                    dve.wait_ge(S("bank0"), ev.banks(0) + 1)
                    ev.take(0)
                    if len(proj) == 1:
                        dve.wait_ge(S("unit1"), ev.take(1) + 1)
                        tt(gt, gt, bank(1, 2, CW), ALU.mult).then_inc(S("bank1"), 1)
                        dve.wait_ge(S("bank1"), ev.banks(1))
                    else:
                        for s in (2, 0, 1):
                            split(s)
                        ev.take(1, False)
                        dve.wait_ge(S("unit2"), ev.take(2, False) + 1)
                        tt(gt, gt, ps[:, 3:5, 0:T], ALU.mult).then_inc(S("q_proj"), 1)
                        dve.wait_ge(S("q_proj"), i + 2)
                    dst = rows(mix, 2 * i, 2)
                    if first:
                        V.tensor_copy(dst, gt).then_inc(S("p_used"), 1)
                    else:
                        tt(dst, dst, gt, ALU.add).then_inc(S("p_used"), 1)
                    if len(proj) == 1:
                        split(1)
                    if last_ is not None:
                        low(2 * i + M0, dst, "mix_hi", i + last_ + 1, "mix_lo")
                return body

            fill = gated(True)
            phase(mlstm, 4, (0, 1, 2, 1), 1 + 3 + 1 + 2)
            for n in range(2):
                loop(gated(False, 0 if n == 1 else None), 4, (0, 1))

            def lower(src, g, b, splits):
                for k in (2 * b, 2 * b + 1):
                    dve.wait_ge(S("n_hi"), KT * splits + k + 1)
                    stt(x_lo[:, H0 + k], src[:, k], pc(g, k), x_hi[:, H0 + k].bitcast(FP32),
                        ALU.mult, ALU.subtract).then_inc(S("n_lo"), 1)

            def four(dst, add, g=None):
                for b, s in enumerate((0, 1, 2, 1)):
                    split((2, 1, 0, 1)[b])
                    dve.wait_ge(S(f"unit{s}"), ev.take(s) + 1)
                    d = dst[:, 2 * b:2 * b + 2]
                    last = tt(d, d, bank(s, 2, CW), ALU.add) if add else V.tensor_copy(d, bank(s, 2, CW))
                    last.then_inc(S(f"bank{s}"), 1)
                    if g is not None:
                        lower(dst, g, b, 0)

            def scaled(n, src, b):
                if b == 0:
                    dve.wait_ge(S("n_r"), n + 1)
                v = slice(2 * b, 2 * b + 2)
                tt(cells(2048, KT, T)[:, v], src[:, v], bc(cells(4096, T), 2), ALU.mult).then_inc(S("n_t"), 1)

            def added(g, b, before):
                dve.wait_ge(S("n_t"), before + b + 1)
                for k in (2 * b, 2 * b + 1):
                    last = stt(res[:, k], cells(2048, KT, T)[:, k], pc(g, k), res[:, k], ALU.mult, ALU.add)
                return last

            four(res, True, "g_mlp")

            def hidden(c0):
                def body(i):
                    for b, s in enumerate((0, 1, 2, 1)):
                        c = 4 * i + b
                        f, q = cells(512 * (b % 2), 2, T), cells(1024 + 512 * (b % 2), 2, T)
                        ev.take(s)
                        dve.wait_ge(S(f"bank{s}"), ev.banks(s))
                        chain(tt(q, f, bc(cells(4096, T), 2), ALU.mult))
                        tt(q, q, f, ALU.mult).then_inc(S("f_sq"), 1)
                        split((2, 1, 0, 1)[b])
                        low(2 * c + U0, q, "f_hi", c + c0 + 1, "f_lo")
                return body

            dve.wait_ge(S("n_r"), 1)
            loop(hidden(0), 4, (0, 1, 2, 1), 4)

            def deep(dst, add, kb, last_=False):
                def body(i):
                    for b in range(2 * kb):
                        s = (0, 1, 2, 1)[b % 4]
                        if not (last_ and b >= 2 * kb - 2):
                            split((2, 1, 0, 1)[b % 4])
                        n = ev.take(s, False)
                        if b % kb == kb - 1:
                            c = b // kb
                            dve.wait_ge(S(f"unit{s}"), n + 1)
                            d, v = rows(dst, 4 * i + 2 * c, 2), ps[:, 3 + 2 * c:5 + 2 * c, 0:T]
                            last = tt(d, d, v, ALU.add) if add else V.tensor_copy(d, v)
                            last.then_inc(S(f"deep{c}"), 1)
                return body

            loop(deep(res, True, 4), 2, (0, 1, 2, 1) * 2, 0, ())

            nt = cells(2048, KT, T)
            scaled(1, res, 0)
            for b in range(4):
                if b < 3:
                    scaled(1, res, b + 1)
                lower(nt, "norm_mix_pre_w_2", b, 1)
            one, acs = cells(6500, T)[0:32], cells(5120, T)[0:32]
            chain(V.memset(one, 1.0))
            dve.wait_ge(S("dt_a"), 1)
            chain(ts(neg_a, neg_a, -1.0, None, ALU.mult))

            def step_sizes():
                dve.wait_ge(S("dt_z"), 1)
                tt(dtz, bank(4, 2, 32), bc(dtb, 2), ALU.add).then_inc(S("dt_b"), 1)
                dve.wait_ge(S("dt_sp"), 1)
                chain(stt(dtc, dtz, 0.0, la, ALU.max, ALU.add))
                tt(la, dtc, bc(neg_a, 2), ALU.mult).then_inc(S("dt_la"), 1)

            def step_sums():
                dve.wait_ge(S("dt_t"), 1)
                V.tensor_tensor_scan(acs, one, bank(5, T)[0:32], 0.0, ALU.mult, ALU.add).then_inc(S("dt_rows"), 1)
                dve.wait_ge(S("dt_ct"), 1)
                ts(nacs, bank(6, 2, 32), -1.0, None, ALU.mult).then_inc(S("dt_col"), 1)

            aq, ak, abias, ap_ = cells(0, 2, T), cells(512, 2, T), cells(1536, 4, 384), cells(3072, 4, 384)

            def att(i, j):
                if i is not None:
                    split(2)
                if j is not None:
                    dve.wait_ge(S("a_bias"), 16 * j + 16)
                    dve.wait_ge(S("a_l"), j + 1)
                    stt(ap_, ps[:, 3:7, 0:384], 0.125, abias, ALU.mult, ALU.add).then_inc(S("a_b"), 1)
                    dve.wait_ge(S("a_b"), j + 1)
                    V.tensor_reduce(ax[:, 0:4], ap_[:, :, 0:P], AXX, ALU.max, negate=True)
                    V.tensor_reduce(ax[:, 4:8], ap_[:, :, P:384], AXX, ALU.max, negate=True)\
                        .then_inc(S("a_mx"), 1)
                if i is not None:
                    evac(0, aq)
                    split(0)
                if j is not None:
                    dve.wait_ge(S("a_p"), j + 1)
                    chain(V.reciprocal(ax[:, 16:24], ax[:, 8:16]))
                    for t, v in enumerate((slice(0, P), slice(P, 384))):
                        r = bc(ax[:, 16 + 4 * t:20 + 4 * t], v.stop - v.start, 2)
                        last = tt(ap_[:, :, v], ap_[:, :, v], r, ALU.mult)
                    last.then_inc(S("a_pn"), 1)
                if i is not None:
                    if j is None:
                        step_sizes()
                    evac(1, ak)
                    split(1)
                    ev.take(2)
                    if j is None:
                        step_sums()
                if j is not None:
                    low(2 * j + YAT, bank(7, 2, T), "a_hi", j + 1, "a_lo")

            phase(att, 3, (0, 1, 2), 1)

            dxp, dcv, dsg, dz = cells(0, 4, 260), cells(1040, 4, T), cells(2064, 4, T), cells(3088, 2, T)
            dab, dcb, dxd, dec, dr, dy = (cells(3600, 4, T), cells(4624, 384), cells(5008, 2, T),
                                          cells(5520, 4, 384), cells(4624, T), cells(7056, 2, T))

            def columns(v, at, n):
                return v[:, at:at + n] if isinstance(at, int) else v[:, bass.ds(at, n)]

            V.memset(dxp[:, :, 0:3], 0.0).then_inc(S("m_pad"), 1)

            def ssm(i, j):
                gates = ev.banks(2)
                if j is not None:
                    dve.wait_ge(S("d_bc"), 16 * j + 16)
                    for h in range(4):
                        for s, (lo, hi, at) in enumerate(((0, T, 0), (P, T, T))):
                            last = ts(dec[:, h, at:at + hi - lo], dab[:, h, lo:hi],
                                      columns(nacs[:, s], 4 * j + h, 1), 0.0, ALU.add, ALU.min)
                    last.then_inc(S("d_d"), 1)
                    if i is None:
                        fill(0)
                    dve.wait_ge(S("d_cb"), j + 1)
                    tt(dcb, bank(3, 384), incl3, ALU.mult)
                    for t in range(2):
                        last = tt(dxd[:, t].rearrange("p (h c) -> p h c", h=4),
                                  bank(4, 2, T)[:, t].rearrange("p (h c) -> p h c", h=4),
                                  bc(columns(dtc[:, t], 4 * j, 4), 64, 2), ALU.mult)
                    chain(last)
                    for c in range(2):
                        ts(dy[:, c], dcv[:, c], columns(skip, 2 * j + c, 1), None, ALU.mult)
                    dve.wait_ge(S("d_e"), j + 1)
                    tt(dec, dec, bc(dcb, 4), ALU.mult).then_inc(S("d_L"), 1)
                if i is not None:
                    split(2)
                    split(0)
                    ev.take(0)
                    evac(1, dxp[:, 2:4, 3:259])
                    ev.take(2)
                if j is not None:
                    if i is None:
                        fill(1)
                    dve.wait_ge(S("d_yp"), j + 1)
                    chain(tt(dy, dy, bank(5, 2, T), ALU.add))
                    dve.wait_ge(S("bank2"), gates)
                    tt(dy, dy, dz, ALU.mult).then_inc(S("d_y"), 1)
                if i is None:
                    fill(2)
                if i is not None:
                    dve.wait_ge(S("d_c0"), i + 1)
                    conv(dxp, dcv, "_2", [2 * i, 2 * i + 1, i + 16, i + 24], 32).then_inc(S("d_cv"), 1)
                if j is not None:
                    dve.wait_ge(S("d_r"), j + 1)
                    for c in range(2):
                        last = stt(dy[:, c], dy[:, c], pc("ssm_norm_w_2", 2 * j + c), dr, ALU.mult, ALU.mult)
                    last.then_inc(S("d_yn"), 1)
                if i is not None:
                    split(1)
                if j is not None:
                    low(2 * j + YSS, dy, "d_hi", j + 1, "d_lo")
                if i is None:
                    fill(3)

            fill = gated(True)
            phase(ssm, 8, (0, 1, 2), 1 + 1 + 2)
            loop(gated(False, 4, (1, 2)), 4, (0, 1, 2), 0, (0,))
            four(mix, False)
            scaled(2, mix, 0)
            for b in range(4):
                if b < 3:
                    scaled(2, mix, b + 1)
                added("norm_mix_post_w_2", b, 4).then_inc(S("r_post"), 1)
                if b > 0:
                    lower(res, "norm_ffn_pre_w_2", b - 1, 2)
            lower(res, "norm_ffn_pre_w_2", 3, 2)
            dve.wait_ge(S("n_r"), 4)
            loop(hidden(16), 4, (0, 1, 2, 1), 4)
            deep(mix, False, 4)(0)
            deep(mix, False, 4, True)(1)
            scaled(4, mix, 0)
            for b in range(4):
                if b < 3:
                    scaled(4, mix, b + 1)
                added("norm_ffn_post_w_2", b, 8).then_inc(S("end"), 1)
            for b in range(2):
                dve.wait_ge(S("end_t"), 2 * b + 1)
                V.tensor_copy(cells(0, 2, D)[:, 0, 512 * b:512 * b + 512], bank(3 + b, 512)).then_inc(S("y_ready"), 1)

        @block.tensor
        def _(pe):
            sl = Slots()
            FP, TOK = False, True

            def mm(o, l, r, start=True, stop=True):
                return nc.tensor.matmul(o, l, r, start=start, stop=stop)

            def tr(o, i):
                return nc.tensor.transpose(o, i, ident[0:i.shape[0], 0:i.shape[0]])

            def unit_half(s, o, at, tok, nk=KT, lo=None):
                last = products(pe, s, o, at, tok, nk, lo=lo)
                if o == 1:
                    last.then_inc(S(f"unit{s}"), 1)

            def unit(s, at, tok=FP, nk=KT, lo=None):
                begin(pe, sl, s)
                unit_half(s, 0, at, tok, nk, lo)
                unit_half(s, 1, at, tok, nk)

            pe.wait_ge(S("cst_in"), 16)
            pe.wait_ge(S("prow_in"), 16 * sum(len(t) for t in PARAM_TILES))
            prow = cells(4096, 3, P)
            for t in range(3):
                last = tr(bank(7, 3, P)[:, t], prow[:, t])
            last.then_inc(S("pcol_t"), 1)
            xn = cells(4480, 2, D)
            mtok, xtok = cells(2048, 2, D), cells(0, 2, D)

            def turned(src, b, name):
                for kt in (2 * b, 2 * b + 1):
                    for t in range(2):
                        last = tr(bank(b, 2, T)[:, kt % 2, t * P:(t + 1) * P], src[:, t, kt * P:(kt + 1) * P])
                last.then_inc(S(name), 1)

            pe.wait_ge(S("xn"), 1)
            for b in range(4):
                turned(xn, b, "h_t")
            pe.wait_ge(S("mn"), 1)
            for b in range(4):
                pe.wait_ge(S("h_lo"), b + 1)
                turned(mtok, b, "h_t")
            for b in range(4):
                pe.wait_ge(S("h_lo"), b + 5)
                turned(xtok, b, "res_t")
            pe.wait_ge(S("gate_in"), 32)
            for t in range(2):
                for k in range(KT):
                    for m, xt in enumerate((x_hi, x_lo)):
                        last = mm(bank(4, 2, 8)[:, t], xt[:, H0 + k, t * P:(t + 1) * P].bitcast(FP32), wif[:, k],
                                  k == 0 and m == 0, k == KT - 1 and m == 1)
            last.then_inc(S("g_z"), 1)
            pe.wait_ge(S("g_lf"), 1)
            for part in range(2):
                for t in range(2):
                    last = tr(bank(5, 2, T)[0:4, part, t * P:(t + 1) * P], gt1[:, t, 4 * part:4 * part + 4])
            last.then_inc(S("g_t"), 1)
            pe.wait_ge(S("g_rows"), 1)
            arow = cells(5632, T)
            for t in range(2):
                last = tr(bank(6, 2, 4)[:, t], arow[0:4, t * P:(t + 1) * P])
            last.then_inc(S("g_ct"), 1)
            pe.wait_ge(S("res"), 4)
            pe.wait_ge(S("g_col"), 1)

            kq, v, sq, kqn, p, pT = (cells(0, 4, T), cells(1024, 2, T), cells(1536, 4, T), cells(3072, 4, T),
                                     cells(4096, 2, T), cells(4608, 2, T))

            def cross(i, j, mem=M0):
                evacuated = [sl.banks(s) for s in range(SLOTS)]
                if i is not None:
                    begin(pe, sl, 0)
                    unit_half(0, 0, mem, FP)
                if j is not None:
                    pe.wait_ge(S("c_sq"), j + 1)
                    for n in range(4):
                        last = mm(bank(3, 2, T)[:, n // 2], ones, sq[:, n], n % 2 == 0, n % 2 == 1)
                    last.then_inc(S("c_ss"), 1)
                if i is not None:
                    unit_half(0, 1, mem, FP)
                    begin(pe, sl, 1)
                    unit_half(1, 0, H0, FP)
                if j is not None:
                    pe.wait_ge(S("c_n"), j + 1)
                    for t in range(2):
                        for d in range(2):
                            last = mm(bank(4, 2, T)[:, t], kqn[:, 2 + d, t * P:(t + 1) * P], kqn[:, d],
                                      d == 0, d == 1)
                    last.then_inc(S("c_lg"), 1)
                if i is not None:
                    unit_half(1, 1, H0, FP)
                    begin(pe, sl, 2)
                    unit_half(2, 0, mem, TOK)
                if j is not None:
                    pe.wait_ge(S("c_pn"), j + 1)
                    for m in range(2):
                        for t in range(2):
                            last = tr(bank(5, 2, T)[:, m, t * P:(t + 1) * P], p[:, t, m * P:(m + 1) * P])
                    last.then_inc(S("c_t"), 1)
                if i is not None:
                    unit_half(2, 1, mem, TOK)
                if j is not None:
                    pe.wait_ge(S("c_pt"), j + 1)
                    need(pe, "bank2", evacuated[2])
                    for d in range(2):
                        for m in range(2):
                            last = mm(bank(6, 2, T)[:, d], v[:, m, d * P:(d + 1) * P], pT[:, m], m == 0, m == 1)
                    last.then_inc(S("c_y"), 1)

            def phase(body, trips, pattern, first=True, last_=True):
                if first:
                    body(0, None)
                sl.enter(pattern, 0)
                with pe.Fori(0, trips - 1) as j:
                    sl.trip = j
                    body(j + 1, j)
                sl.leave(trips - 1)
                if last_:
                    body(None, trips - 1)

            phase(cross, 4, (0, 1, 2), last_=False)
            cross(4, 3, H0)

            sq_, sk_, sv_ = cells(0, 2, T), cells(512, 2, T), cells(1024, 2, T)
            sn, sA = cells(3072, 2, 384), cells(2304, 2, 384)

            def stick(i, j):
                evacuated = [sl.banks(s) for s in range(SLOTS)]
                if i is not None:
                    begin(pe, sl, 0)
                    unit_half(0, 0, H0, FP)
                if j is not None:
                    need(pe, "bank0", evacuated[0])
                    need(pe, "bank1", evacuated[1])
                    for h in range(2):
                        mm(bank(3 + h, 384)[:, 0:T], sk_[:, h, 0:P], sq_[:, h, :])
                        last = mm(bank(3 + h, 384)[:, T:384], sk_[:, h, P:T], sq_[:, h, P:T])
                    last.then_inc(S("s_z"), 1)
                if i is not None:
                    unit_half(0, 1, H0, FP)
                    begin(pe, sl, 1)
                    unit_half(1, 0, H0, FP)
                    unit_half(1, 1, H0, FP)
                if j is not None:
                    pe.wait_ge(S("s_nm"), j + 1)
                    for h in range(2):
                        mm(bank(5 + h, 384)[:, 0:T], later, sn[:, h, 0:T], True, False)
                        mm(bank(5 + h, 384)[:, P:T], ones, sn[:, h, T:384], False, True)
                        last = mm(bank(5 + h, 384)[:, T:384], later, sn[:, h, T:384])
                    last.then_inc(S("s_lt"), 1)
                if i is not None:
                    begin(pe, sl, 2)
                    unit_half(2, 0, H0, TOK)
                    unit_half(2, 1, H0, TOK)
                if j is not None:
                    pe.wait_ge(S("s_Am"), j + 1)
                    need(pe, "bank2", evacuated[2])
                    for h in range(2):
                        mm(bank(7, 2, T)[:, h], sv_[:, 0, h * P:(h + 1) * P], sA[:, h, 0:T], True, False)
                        last = mm(bank(7, 2, T)[:, h, P:T], sv_[:, 1, h * P:(h + 1) * P], sA[:, h, T:384],
                                  False, True)
                    last.then_inc(S("s_y"), 1)

            phase(stick, 4, (0, 1, 2), first=False)

            cv, mv, w_, sc, msq = cells(1040, 4, T), cells(3088, 2, T), cells(4624, 384), cells(5008, 384), \
                cells(6160, 2, T)

            def mlstm(i, j):
                evacuated = [sl.banks(s) for s in range(SLOTS)]
                if i is not None:
                    begin(pe, sl, 0)
                    unit_half(0, 0, H0, FP)
                    unit_half(0, 1, H0, FP)
                if i is None:
                    fill(0)
                if j is not None:
                    pe.wait_ge(S("m_qk"), j + 1)
                    for d in range(2):
                        mm(bank(3, 384)[:, 0:T], cv[:, 2 + d, 0:P], cv[:, d, :], d == 0, d == 1)
                    for d in range(2):
                        last = mm(bank(3, 384)[:, T:384], cv[:, 2 + d, P:T], cv[:, d, P:T], d == 0, d == 1)
                    last.then_inc(S("m_s"), 1)
                if i is not None:
                    begin(pe, sl, 1)
                    unit_half(1, 0, H0, FP)
                    unit_half(1, 1, H0, FP)
                    begin(pe, sl, 2)
                    unit_half(2, 0, H0, TOK)
                if i is None:
                    fill(1)
                if j is not None:
                    pe.wait_ge(S("m_sc"), j + 1)
                    need(pe, "bank2", evacuated[2])
                    mm(bank(4, T), ones, sc[:, 0:T], True, False)
                    mm(bank(4, T)[:, P:T], ones, sc[:, T:384], False, True).then_inc(S("m_den"), 1)
                    for d in range(2):
                        mm(bank(5, 2, T)[:, d], mv[:, 0, d * P:(d + 1) * P], sc[:, 0:T], True, False)
                        last = mm(bank(5, 2, T)[:, d, P:T], mv[:, 1, d * P:(d + 1) * P], sc[:, T:384], False, True)
                    last.then_inc(S("m_num"), 1)
                if i is not None:
                    unit_half(2, 1, H0, TOK)
                    begin(pe, sl, 1)
                    unit_half(1, 0, H0, FP)
                if i is None:
                    fill(2)
                if j is not None:
                    pe.wait_ge(S("m_sq"), j + 1)
                    for d in range(2):
                        last = mm(bank(6, T), ones, msq[:, d], d == 0, d == 1)
                    last.then_inc(S("m_ss"), 1)
                if i is not None:
                    unit_half(1, 1, H0, FP)
                else:
                    fill(3)

            def loop(body, trips, pattern, filled=None):
                sl.enter(pattern, 0, filled)
                with pe.Fori(0, trips) as i:
                    sl.trip = i
                    body(i)
                sl.leave(trips)

            def gated(at):
                def body(i):
                    unit(0, H0)
                    unit(1, at)
                return body

            fill = gated(YX)
            pe.wait_ge(S("c_lo"), 4)
            phase(mlstm, 4, (0, 1, 2, 1))
            for n, at in enumerate((YSB, YML)):
                pe.wait_ge(S(("s_lo", "m_lo")[n]), 4)
                loop(gated(at), 4, (0, 1))

            def norm(n, pairs=range(4)):
                for b in pairs:
                    pe.wait_ge(S("n_sq"), 4 * n + b + 1)
                    for k in (2 * b, 2 * b + 1):
                        last = mm(bank(7, T), ones, cells(SQ, KT, T)[:, k], k == 0, k == KT - 1)
                if b == 3:
                    last.then_inc(S("n_ss"), 1)

            def four(at, lo):
                def body(i):
                    for b, s in enumerate((0, 1, 2, 1)):
                        unit(s, at, lo=lo if b == 0 else None)
                return body

            def four_normed(at, n, lo):
                for b, s in enumerate((0, 1, 2, 1)):
                    unit(s, at, lo=lo if b == 0 else None)
                    if b:
                        norm(n, (b - 1,))
                norm(n, (3,))

            def deep(kb, at, done0):
                def body(i):
                    for b in range(2 * kb):
                        s, c = (0, 1, 2, 1)[b % 4], b // kb
                        pe.wait_ge(S(f"w_split{s}"), sl.take(s, False) + 1)
                        pe.wait_ge(S("f_lo"), 8 * done0 + KT // 2 * (b % kb + 1))
                        if b % kb == 0:
                            pe.wait_ge(S(f"deep{c}"), i + done0 + 1)
                        for o in range(2):
                            last = products(pe, s, o, at + KT * (b % kb), FP, out_=bank(3 + 2 * c + o, T),
                                            start=b % kb == 0, stop=b % kb == kb - 1)
                        last.then_inc(S(f"unit{s}"), 1)
                return body

            four_normed(M0, 0, ("mix_lo", 0, 2))
            loop(four(H0, ("n_lo", 0, 1)), 4, (0, 1, 2, 1))
            loop(deep(4, U0, 0), 2, (0, 1, 2, 1) * 2, ())

            norm(1)

            def step_sizes():
                pe.wait_ge(S("dt_in"), 80)
                for t in range(2):
                    for k in range(KT):
                        for m, xt in enumerate((x_hi, x_lo)):
                            last = mm(bank(4, 2, 32)[:, t], xt[:, H0 + k, t * P:(t + 1) * P].bitcast(FP32),
                                      wdt[:, k], k == 0 and m == 0, k == KT - 1 and m == 1)
                last.then_inc(S("dt_z"), 1)

            def step_rows():
                pe.wait_ge(S("dt_la"), 1)
                for t in range(2):
                    last = tr(bank(5, T)[0:32, t * P:(t + 1) * P], la[:, t])
                last.then_inc(S("dt_t"), 1)

            def step_columns():
                pe.wait_ge(S("dt_rows"), 1)
                for t in range(2):
                    last = tr(bank(6, 2, 32)[:, t], cells(5120, T)[0:32, t * P:(t + 1) * P])
                last.then_inc(S("dt_ct"), 1)

            aq, ak, av, ap_, apT = (cells(0, 2, T), cells(512, 2, T), cells(1024, 2, T), cells(3072, 4, 384),
                                    cells(4608, 4, 384))

            def head(h):
                return slice(64 * (h % 2), 64 * (h % 2) + 64), h // 2

            def att(i, j):
                evacuated = [sl.banks(s) for s in range(SLOTS)]
                if i is not None:
                    begin(pe, sl, 0)
                    unit_half(0, 0, H0, FP, lo=("n_lo", KT, 1) if j is None else None)
                if j is not None:
                    pe.wait_ge(S("dt_col"), 1)
                    need(pe, "bank0", evacuated[0])
                    need(pe, "bank1", evacuated[1])
                    for h in range(4):
                        o, c = head(h)
                        mm(bank(3 + h, 384)[:, 0:P], aq[o, c, 0:P], ak[o, c, 0:P])
                        last = mm(bank(3 + h, 384)[:, P:384], aq[o, c, P:T], ak[o, c, :])
                    last.then_inc(S("a_l"), 1)
                if i is None:
                    unit(0, H0)
                if i is not None:
                    unit_half(0, 1, H0, FP)
                    if j is None:
                        step_sizes()
                    begin(pe, sl, 1)
                    unit_half(1, 0, H0, FP)
                    unit_half(1, 1, H0, FP)
                    if j is None:
                        step_rows()
                if j is not None:
                    pe.wait_ge(S("a_pn"), j + 1)
                    for h in range(4):
                        for b in range(3):
                            last = tr(bank(3 + h, 384)[:, b * P:(b + 1) * P], ap_[:, h, b * P:(b + 1) * P])
                    last.then_inc(S("a_t"), 1)
                if i is None:
                    unit(1, H0)
                if i is not None:
                    begin(pe, sl, 2)
                    unit_half(2, 0, H0, TOK)
                    unit_half(2, 1, H0, TOK)
                    if j is None:
                        step_columns()
                if j is not None:
                    pe.wait_ge(S("a_pt"), j + 1)
                    need(pe, "bank2", evacuated[2])
                    for h in range(4):
                        o, c = head(h)
                        mm(bank(7, 2, T)[o, c], av[:, 0, 64 * h:64 * h + 64], apT[:, h, 0:T], True, False)
                        last = mm(bank(7, 2, T)[o, c, P:T], av[:, 1, 64 * h:64 * h + 64], apT[:, h, T:384],
                                  False, True)
                    last.then_inc(S("a_y"), 1)

            phase(att, 3, (0, 1, 2))

            dcv, dxd, dec, dsq = cells(1040, 4, T), cells(5008, 2, T), cells(5520, 4, 384), cells(5520, 2, T)

            def ssm(i, j):
                if i is not None and j is not None:
                    begin(pe, sl, 0)
                    unit_half(0, 0, H0, FP)
                    unit_half(0, 1, H0, FP)
                if i is None:
                    fill(0)
                if j is not None:
                    pe.wait_ge(S("d_xc"), j + 1)
                    mm(bank(3, 384)[:, 0:T], dcv[:, 2, 0:P], dcv[:, 3, :])
                    mm(bank(3, 384)[:, T:384], dcv[:, 2, P:T], dcv[:, 3, P:T])
                    for t in range(2):
                        for c in range(2):
                            last = tr(bank(4, 2, T)[:, t, c * P:(c + 1) * P], dcv[:, c, t * P:(t + 1) * P])
                    last.then_inc(S("d_cb"), 1)
                if i is not None and j is not None:
                    begin(pe, sl, 1)
                    unit_half(1, 0, H0, FP)
                    unit_half(1, 1, H0, FP)
                if i is None:
                    fill(1)
                if j is not None:
                    pe.wait_ge(S("d_L"), j + 1)
                    for h in range(4):
                        o, c = head(h)
                        mm(bank(5, 2, T)[o, c], dxd[:, 0, 64 * h:64 * h + 64], dec[:, h, 0:T], True, False)
                        last = mm(bank(5, 2, T)[o, c, P:T], dxd[:, 1, 64 * h:64 * h + 64], dec[:, h, T:384],
                                  False, True)
                    last.then_inc(S("d_yp"), 1)
                if i is not None:
                    begin(pe, sl, 2)
                    unit_half(2, 0, H0, FP)
                if i is None:
                    fill(2)
                if j is not None:
                    pe.wait_ge(S("d_sq"), j + 1)
                    for c in range(2):
                        last = mm(bank(6, T), ones, dsq[:, c], c == 0, c == 1)
                    last.then_inc(S("d_ss"), 1)
                if i is not None:
                    unit_half(2, 1, H0, FP)
                else:
                    fill(3)

            def gated_att(i):
                pe.wait_ge(S("a_lo"), 3)
                unit(0, H0)
                unit(1, YAT, FP, 6)

            fill = gated_att
            phase(ssm, 8, (0, 1, 2))

            def gated_ssm(i):
                unit(0, H0)
                pe.wait_ge(S("q_proj"), i + 1)
                for kb in range(2):
                    pe.wait_ge(S(f"w_split{1 + kb}"), sl.take(1 + kb, False) + 1)
                    for o in range(2):
                        last = products(pe, 1 + kb, o, YSS + KT * kb, FP, out_=bank(3 + o, T),
                                        start=kb == 0, stop=kb == 1)
                    last.then_inc(S(f"unit{1 + kb}"), 1)

            pe.wait_ge(S("d_lo"), 8)
            loop(gated_ssm, 4, (0, 1, 2), (0,))
            four_normed(M0, 2, ("mix_lo", 4, 2))
            norm(3)
            loop(four(H0, ("n_lo", 2 * KT, 1)), 4, (0, 1, 2, 1))
            loop(deep(4, U0, 2), 2, (0, 1, 2, 1) * 2, ())
            norm(4)
            for b in range(2):
                pe.wait_ge(S("end"), 2 * b + 2)
                for t in range(2):
                    for k in range(4):
                        last = tr(bank(3 + 2 * t + b, 4, P)[:, k], res[:, 4 * b + k, t * P:(t + 1) * P])
                    last.then_inc(S("end_t"), 1)


INPUTS = ("x", "mem", "g_mix", "w_in", "b_if", "b_gate", "conv_w", "conv_b", "ml_norm_g", "g_mem", "w_mem_kv",
          "q_norm_g", "k_norm_g", "w_sb_proj", "w_ml_proj", "w_x_proj", "w_out", "g_mlp", "w_ff1", "w_ff2",
          "norm_mix_pre_w_2", "w_in_2", "b_gate_2", "conv_w_2", "conv_b_2", "dt_bias_2", "a_log_2", "d_skip_2",
          "ssm_norm_w_2", "w_att_proj_2", "w_ssm_proj_2", "w_out_2", "norm_mix_post_w_2", "norm_ffn_pre_w_2",
          "w_up_2", "w_down_2", "norm_ffn_post_w_2")


def constants():
    import numpy as np
    p, f = np.arange(P)[:, None], np.arange(P)[None, :]
    one = np.ones((P, P))
    table = np.concatenate([p == f, one, p > f, f > p, one, f > p, f >= p, one, f >= p], 1)
    first = [2.0 ** (-(i + 1)) for i in range(8)]
    slopes = np.array(first + [2.0 ** (-0.5 * (i + 1)) for i in range(0, 8, 2)], np.float32)
    dist = np.arange(T)[:, None] - np.arange(T)[None, :]
    held = (dist >= 0) * ((dist <= 128) * 1 + (dist % 4 == 0) + (dist % 16 == 0))
    count = np.where(held > 0, np.log(np.maximum(held, 1)), -1e30)
    bias = -slopes[:, None, None].astype(np.float64) * np.maximum(dist, 0) + count
    bias = np.concatenate([bias[:, :P, :P], bias[:, P:, :]], 2)
    return (np.ascontiguousarray(table, dtype=np.float32),
            np.ascontiguousarray(bias.transpose(1, 0, 2), dtype=np.float32))


def kernel(**inputs):
    import numpy as np
    import concourse.bacc as bacc
    from concourse.bass_utils import run_bass_kernel_spmd as run

    nc = bacc.Bacc("TRN2", target_bir_lowering=False, num_devices=1)
    arrays, a = {}, {}
    given = {name: np.ascontiguousarray(inputs[name]) for name in INPUTS}
    given["consts"], given["att_bias"] = constants()
    for name, v in given.items():
        arrays[f"in_{name}"] = v
        a[name] = nc.dram_tensor(f"in_{name}", v.shape, mybir.dt.from_np(v.dtype), kind="ExternalInput").ap()
    a["rows"] = nc.dram_tensor("rows", (3, 32, T), FP32, kind="Internal").ap()
    out = nc.dram_tensor("out_0_dram", (1, T, D), FP32, kind="ExternalOutput").ap()
    build(nc, a, out)
    r = run(nc, [arrays], core_ids=[0])
    return r.results[0]["out_0_dram"]
```
